# Optimizing a Trainium2 kernel written in Bass

```python
import math
import jax, jax.numpy as jnp
from jax import lax
import numpy as np

D_MODEL = 2048
BATCH = 1
SEQ = 1024
DEPTH = 1
DEC_BATCH = 8
DEC_SEQ = 1
PAST_LEN = 256
PAGE_SIZE = 128

SSM_WIDTH = D_MODEL // 2
SSM_GROUP_SIZE = 16
SSM_GROUPS = SSM_WIDTH // SSM_GROUP_SIZE
SSM_STATE = 64
DT_MIN = 1e-3
DT_MAX = 1e-1
SB_HEAD_DIM = 128
SB_WIDTH = D_MODEL // 2
SB_HEADS = SB_WIDTH // SB_HEAD_DIM
SB_SCALE = 1.0 / math.sqrt(SB_HEAD_DIM)
SB_BIAS_LO = -7.0
SB_BIAS_HI = -5.0
Q_BLOCK = 128
RMS_EPS = 1e-6
SPLITS = (SSM_WIDTH, 2 * SSM_WIDTH, 2 * SSM_WIDTH + SB_WIDTH, 2 * SSM_WIDTH + 2 * SB_WIDTH,
          2 * SSM_WIDTH + 3 * SB_WIDTH, 2 * SSM_WIDTH + 4 * SB_WIDTH,
          2 * SSM_WIDTH + 4 * SB_WIDTH + D_MODEL)
N_IN = 2 * SSM_WIDTH + 4 * SB_WIDTH + 2 * D_MODEL

kernel_name = 'hybrid_s5_stickbreaking_gated_step'

def rmsnorm(x, g):
    xf = x.astype(jnp.float32)
    y = xf * lax.rsqrt(jnp.mean(xf * xf, axis=-1, keepdims=True) + RMS_EPS)
    return (y * g.astype(jnp.float32)).astype(x.dtype)

def s5_scan(u, h0, A_re, A_im, log_dt, B_re, B_im, C_re, C_im, D):
    f32 = jnp.float32
    b, L, _ = u.shape
    uf = u.astype(f32).reshape(b, L, SSM_GROUPS, SSM_GROUP_SIZE)
    lam = lax.complex(A_re.astype(f32), A_im.astype(f32))
    dt = jnp.exp(log_dt.astype(f32))[:, None]
    a_bar = jnp.exp(lam * dt)
    b_bar = ((a_bar - 1.0) / lam)[:, :, None] * lax.complex(B_re.astype(f32), B_im.astype(f32))
    bu = jnp.einsum('blgc,gpc->blgp', uf.astype(jnp.complex64), b_bar)
    bu = bu.at[:, 0].add(a_bar[None] * h0)
    a_seq = jnp.broadcast_to(a_bar, bu.shape)

    def combine(left, right):
        a_l, b_l = left
        a_r, b_r = right
        return a_l * a_r, a_r * b_l + b_r

    _, h = lax.associative_scan(combine, (a_seq, bu), axis=1)
    c = lax.complex(C_re.astype(f32), C_im.astype(f32))
    y = jnp.real(jnp.einsum('blgp,gcp->blgc', h, c)) + D.astype(f32).reshape(SSM_GROUPS, SSM_GROUP_SIZE) * uf
    return y.reshape(b, L, SSM_WIDTH), h[:, -1]

def sb_block(q_blk, pos_blk, k, v, k_pos, bias):
    z = jnp.einsum('bqhd,bkhd->bhqk', q_blk.astype(jnp.float32), k) * SB_SCALE + bias[None, :, None, None]
    valid = k_pos[None, :] < pos_blk[:, None]
    log_keep = jnp.where(valid, -jax.nn.softplus(z), 0.0)
    later = lax.cumsum(log_keep, axis=3, reverse=True) - log_keep
    w = jnp.where(valid, jnp.exp(jax.nn.log_sigmoid(z) + later), 0.0)
    return jnp.einsum('bhqk,bkhd->bqhd', w, v)

def sb_sweep(q, k, v, q_pos, k_pos, bias):
    b, lq, h, d = q.shape
    qb = min(Q_BLOCK, lq)
    nb = -(-lq // qb)
    pad = nb * qb - lq
    qp = jnp.pad(q, ((0, 0), (0, pad), (0, 0), (0, 0)))
    pp = jnp.pad(q_pos, (0, pad))
    q_blocks = qp.reshape(b, nb, qb, h, d).transpose(1, 0, 2, 3, 4)
    pos_blocks = pp.reshape(nb, qb)
    kf = k.astype(jnp.float32)
    vf = v.astype(jnp.float32)
    bf = bias.astype(jnp.float32)
    o = lax.map(lambda blk: sb_block(blk[0], blk[1], kf, vf, k_pos, bf), (q_blocks, pos_blocks))
    o = o.transpose(1, 0, 2, 3, 4).reshape(b, nb * qb, h, d)[:, :lq]
    return o.astype(q.dtype)

def mixer_layer(x, h0, past_k, past_v, q_pos, k_pos, p):
    (norm_g, w_in, A_re, A_im, log_dt, B_re, B_im, C_re, C_im, D,
     glu_w, glu_b, sb_bias, w_branch_a, w_branch_b, w_out) = p
    b, L, _ = x.shape
    xn = rmsnorm(x, norm_g)
    proj = xn @ w_in
    u_a, z_a, q, k, v, z_b, g_a, g_b = jnp.split(proj, SPLITS, axis=-1)
    y_a, h_last = s5_scan(u_a, h0, A_re, A_im, log_dt, B_re, B_im, C_re, C_im, D)
    y_a = jax.nn.gelu(y_a, approximate=False)
    y_a = y_a * jax.nn.sigmoid(y_a @ glu_w.astype(jnp.float32) + glu_b.astype(jnp.float32))
    y_a = y_a.astype(x.dtype) * jax.nn.silu(z_a)
    q = q.reshape(b, L, SB_HEADS, SB_HEAD_DIM)
    k = k.reshape(b, L, SB_HEADS, SB_HEAD_DIM)
    v = v.reshape(b, L, SB_HEADS, SB_HEAD_DIM)
    k_all = jnp.concatenate([past_k.astype(k.dtype), k], axis=1)
    v_all = jnp.concatenate([past_v.astype(v.dtype), v], axis=1)
    o = sb_sweep(q, k_all, v_all, q_pos, k_pos, sb_bias).reshape(b, L, SB_WIDTH) * jax.nn.silu(z_b)
    merged = jax.nn.sigmoid(g_a) * (y_a @ w_branch_a) + jax.nn.sigmoid(g_b) * (o @ w_branch_b)
    return x + merged @ w_out, k, v, h_last

def setup_inputs(seed: int = 0) -> dict:
    key = jax.random.key(seed)
    ks = jax.random.split(key, 24)
    f32 = jnp.float32
    n_pages = PAST_LEN // PAGE_SIZE
    n_phys = (DEC_BATCH * n_pages * 5) // 4

    def nrm(k, shape, scale):
        return jax.random.normal(k, shape, f32) * scale

    x_prompt = nrm(ks[0], (BATCH, SEQ, D_MODEL), 1.0)
    x_sample = nrm(ks[1], (DEC_BATCH, DEC_SEQ, D_MODEL), 1.0)
    cache_k = nrm(ks[2], (DEPTH, n_phys, PAGE_SIZE, SB_HEADS, SB_HEAD_DIM), 1.0)
    cache_v = nrm(ks[3], (DEPTH, n_phys, PAGE_SIZE, SB_HEADS, SB_HEAD_DIM), 1.0)
    state_ssm_re = nrm(ks[4], (DEPTH, DEC_BATCH, SSM_GROUPS, SSM_STATE), 0.1)
    state_ssm_im = nrm(ks[5], (DEPTH, DEC_BATCH, SSM_GROUPS, SSM_STATE), 0.1)
    page_table = jax.random.permutation(ks[6], n_phys)[: DEC_BATCH * n_pages].reshape(DEC_BATCH, n_pages).astype(jnp.int32)
    norm_g = 1.0 + nrm(ks[7], (DEPTH, D_MODEL), 0.02)
    w_in = nrm(ks[8], (DEPTH, D_MODEL, N_IN), D_MODEL ** -0.5)
    n = jnp.arange(SSM_STATE, dtype=f32)
    ssm_A_re = -0.5 + nrm(ks[9], (DEPTH, SSM_GROUPS, SSM_STATE), 0.01)
    ssm_A_im = math.pi * n + nrm(ks[10], (DEPTH, SSM_GROUPS, SSM_STATE), 0.01)
    ssm_log_dt = jax.random.uniform(ks[11], (DEPTH, SSM_GROUPS), f32, math.log(DT_MIN), math.log(DT_MAX))
    ssm_B_re = nrm(ks[12], (DEPTH, SSM_GROUPS, SSM_STATE, SSM_GROUP_SIZE), (2 * SSM_GROUP_SIZE) ** -0.5)
    ssm_B_im = nrm(ks[13], (DEPTH, SSM_GROUPS, SSM_STATE, SSM_GROUP_SIZE), (2 * SSM_GROUP_SIZE) ** -0.5)
    ssm_C_re = nrm(ks[14], (DEPTH, SSM_GROUPS, SSM_GROUP_SIZE, SSM_STATE), (2 * SSM_STATE) ** -0.5)
    ssm_C_im = nrm(ks[15], (DEPTH, SSM_GROUPS, SSM_GROUP_SIZE, SSM_STATE), (2 * SSM_STATE) ** -0.5)
    ssm_D = nrm(ks[16], (DEPTH, SSM_WIDTH), 1.0)
    glu_w = nrm(ks[17], (DEPTH, SSM_WIDTH, SSM_WIDTH), SSM_WIDTH ** -0.5)
    glu_b = nrm(ks[18], (DEPTH, SSM_WIDTH), 0.01)
    sb_bias = jax.random.uniform(ks[23], (DEPTH, SB_HEADS), f32, SB_BIAS_LO, SB_BIAS_HI)
    w_branch_a = nrm(ks[19], (DEPTH, SSM_WIDTH, D_MODEL), SSM_WIDTH ** -0.5)
    w_branch_b = nrm(ks[20], (DEPTH, SB_WIDTH, D_MODEL), SB_WIDTH ** -0.5)
    w_out = nrm(ks[21], (DEPTH, D_MODEL, D_MODEL), D_MODEL ** -0.5)
    norm_f = 1.0 + nrm(ks[22], (D_MODEL,), 0.02)
    return {'x_prompt': x_prompt, 'x_sample': x_sample, 'cache_k': cache_k, 'cache_v': cache_v,
            'state_ssm_re': state_ssm_re, 'state_ssm_im': state_ssm_im, 'page_table': page_table,
            'norm_g': norm_g, 'w_in': w_in, 'ssm_A_re': ssm_A_re, 'ssm_A_im': ssm_A_im,
            'ssm_log_dt': ssm_log_dt, 'ssm_B_re': ssm_B_re, 'ssm_B_im': ssm_B_im,
            'ssm_C_re': ssm_C_re, 'ssm_C_im': ssm_C_im, 'ssm_D': ssm_D, 'glu_w': glu_w, 'glu_b': glu_b,
            'sb_bias': sb_bias, 'w_branch_a': w_branch_a, 'w_branch_b': w_branch_b, 'w_out': w_out,
            'norm_f': norm_f}

def reference(x_prompt, x_sample, cache_k, cache_v, state_ssm_re, state_ssm_im, page_table,
              norm_g, w_in, ssm_A_re, ssm_A_im, ssm_log_dt, ssm_B_re, ssm_B_im, ssm_C_re, ssm_C_im,
              ssm_D, glu_w, glu_b, sb_bias, w_branch_a, w_branch_b, w_out, norm_f):
    f32 = jnp.float32
    bp, seq = x_prompt.shape[0], x_prompt.shape[1]
    dec_b, dec_seq = x_sample.shape[0], x_sample.shape[1]
    n_pages = page_table.shape[1]
    past_len = n_pages * cache_k.shape[2]
    q_pos_p = jnp.arange(seq, dtype=jnp.int32)
    k_pos_p = q_pos_p
    q_pos_s = past_len + jnp.arange(dec_seq, dtype=jnp.int32)
    k_pos_s = jnp.arange(past_len + dec_seq, dtype=jnp.int32)
    hp, hs = x_prompt, x_sample
    kp_l, vp_l, ks_l, vs_l = [], [], [], []
    srp_l, sip_l, srs_l, sis_l = [], [], [], []
    for l in range(DEPTH):
        p = (norm_g[l], w_in[l], ssm_A_re[l], ssm_A_im[l], ssm_log_dt[l], ssm_B_re[l], ssm_B_im[l],
             ssm_C_re[l], ssm_C_im[l], ssm_D[l], glu_w[l], glu_b[l], sb_bias[l],
             w_branch_a[l], w_branch_b[l], w_out[l])
        h0_p = jnp.zeros((bp, SSM_GROUPS, SSM_STATE), jnp.complex64)
        empty = jnp.zeros((bp, 0, SB_HEADS, SB_HEAD_DIM), x_prompt.dtype)
        hp, kp, vp, sp = mixer_layer(hp, h0_p, empty, empty, q_pos_p, k_pos_p, p)
        past_k = cache_k[l][page_table].reshape(dec_b, past_len, SB_HEADS, SB_HEAD_DIM)
        past_v = cache_v[l][page_table].reshape(dec_b, past_len, SB_HEADS, SB_HEAD_DIM)
        h0_s = lax.complex(state_ssm_re[l].astype(f32), state_ssm_im[l].astype(f32))
        hs, ks_, vs_, ss = mixer_layer(hs, h0_s, past_k, past_v, q_pos_s, k_pos_s, p)
        kp_l.append(kp)
        vp_l.append(vp)
        ks_l.append(ks_)
        vs_l.append(vs_)
        srp_l.append(jnp.real(sp))
        sip_l.append(jnp.imag(sp))
        srs_l.append(jnp.real(ss))
        sis_l.append(jnp.imag(ss))
    y_prompt = rmsnorm(hp, norm_f)
    y_sample = rmsnorm(hs, norm_f)
    k_prompt = jnp.stack(kp_l, axis=0)
    v_prompt = jnp.stack(vp_l, axis=0)
    k_sample = jnp.stack(ks_l, axis=0)
    v_sample = jnp.stack(vs_l, axis=0)
    ssm_re_prompt = jnp.stack(srp_l, axis=0)
    ssm_im_prompt = jnp.stack(sip_l, axis=0)
    ssm_re_sample = jnp.stack(srs_l, axis=0)
    ssm_im_sample = jnp.stack(sis_l, axis=0)
    return (y_prompt, y_sample, k_prompt, v_prompt, k_sample, v_sample,
            ssm_re_prompt, ssm_im_prompt, ssm_re_sample, ssm_im_sample)


_drawn_inputs = setup_inputs


def setup_inputs(seed=0):
    import zlib

    import numpy as np

    out = dict(_drawn_inputs(seed))
    spreads = {}
    factors = {'norm_g': 2.775,
     'ssm_A_re': 16.585,
     'ssm_C_re': 8.0,
     'ssm_C_im': 7.305,
     'glu_b': 25.039,
     'sb_bias': 4.656,
     'norm_f': 7.849,
     'cache_k': 8.0,
     'cache_v': 8.0}
    for name, (base, spread) in spreads.items():
        noise = np.random.default_rng([zlib.crc32(name.encode()), seed]).standard_normal(out[name].shape)
        drawn = base * np.exp(spread * noise) if base else spread * noise
        out[name] = __import__('jax').numpy.asarray(drawn.astype(out[name].dtype))
    for name, factor in factors.items():
        out[name] = (out[name] * factor).astype(out[name].dtype)
    return out
```

```python
import math

import numpy as np

import concourse.bass as bass
from concourse import mybir

F32 = mybir.dt.float32
F32R = mybir.dt.float32r
I32 = mybir.dt.int32
ALU = mybir.AluOpType
ACT = mybir.ActivationFunctionType
AX = mybir.AxisListType

P = 128
D_MODEL, SEQ, NEW = 2048, 1024, 8
TOK = SEQ + NEW
WIDTH = D_MODEL // 2
HEADS, HEAD = 8, 128
GROUPS, GC, STATE = 64, 16, 64
N_PAGES, PAGE = 2, 128
KT = D_MODEL // P
CK = 8
FT = WIDTH // P
NB = 3
NC = TOK // NB
CH = 8
NCH = SEQ // CH
HG = 4
EPS = 1e-6
SCALE = 1.0 / math.sqrt(HEAD)
NEG = -1e30
WORK = 10400
POOL_HALF = 133
DVE_A = 33

TILES = 10
CHUNKS = 2 * TILES
PTS = 8 * TILES
U, ZA, GB0, Q, K, V, ZB, GB1, GA0, GA1 = range(TILES)


def weight_column(tile, i):
    at = {U: 0, ZA: 1, Q: 2, K: 3, V: 4, ZB: 5}
    if tile in at:
        return at[tile] * WIDTH + i * P
    base = 6 * WIDTH + (D_MODEL if tile in (GB0, GB1) else 0)
    return base + i * 2 * P + (P if tile in (GA1, GB1) else 0)


class Carve:

    def __init__(self, buf):
        self.buf, self.at = buf, 0

    def take(self, cols, parts=P):
        a = self.buf[0:parts, self.at:self.at + cols]
        self.at += cols
        assert self.at <= WORK, self.at
        return a


class Chain:

    def __init__(self, eng, sem, base=0):
        self.eng, self.sem, self.base, self.n = eng, sem, base, 0

    def __call__(self, *instructions):
        for ins in instructions:
            self.n += 1
            ins.then_inc(self.sem, 1)
        self.eng.wait_ge(self.sem, self.base + self.n)


def build(stack, nc, x_prompt, x_sample, cache_k, cache_v, st_re, st_im, page_table, norm_g, w_in, A_re, A_im, log_dt,
          B_re, B_im, C_re, C_im, Dw, glu_w, glu_b, sb_bias, w_a, w_b, w_out, norm_f,
          y_prompt, y_sample, k_prompt, v_prompt, k_sample, v_sample, re_prompt, im_prompt, re_sample, im_sample):
    def sb(name, shape, dt=F32):
        return nc.alloc_sbuf_tensor(name, shape, dt)

    def sem(name):
        return nc.alloc_semaphore(name)

    def dram(name, shape):
        return nc.dram_tensor(name, shape, F32, kind="Internal").ap()

    XH, XL = sb("x_high", [P, KT, TOK], F32R), sb("x_low", [P, KT, TOK], F32R)
    raw = [sb(f"w_raw{b}", [P, CK, P]) for b in range(2)]
    hi = [sb(f"w_high{b}", [P, CK, P], F32R) for b in range(2)]
    lo = [sb(f"w_low{b}", [P, CK, P], F32R) for b in range(2)]
    stage = [sb(f"stage{b}", [P, TOK]) for b in range(2)]
    work = sb("work", [P, WORK])
    ident = sb("ident", [P, P])
    negid = sb("neg_ident", [64, 64])
    cmask = sb("causal_mask", [P, P])
    tab = sb("s5_tables", [P, 7, GROUPS])
    dcol, bias_all, nglub = sb("d_col", [P, FT]), sb("sb_bias_all", [P, HEADS]), sb("neg_glu_b", [P, FT])
    szb_s = sb("silu_zb_new", [P, HEADS, NEW])
    bias64 = sb("bias_rows", [HEADS * NEW, 1])
    stat = sb("norm_stats", [P, 8])
    outs_new = sb("out_new_T", [P, KT, NEW])
    ssum, hvar_t, rstd4, w4 = sb("h_squares", [P, 4, KT]), sb("h_variance", [P, 4]), sb("h_rstd", [P, 4]), sb("newton", [P, 4])
    hvar = hvar_t[:, :]
    zero1 = sb("zero1", [P, 1])
    pages = sb("pages", [1, NEW * N_PAGES], I32)
    acc = [nc.alloc_psum_tensor(f"acc{s}", [P, NB, 512], F32) for s in range(2)]
    side = nc.alloc_psum_tensor("side", [P, 2, 512], F32)
    side_flat = side[:, :, :].rearrange("p a b -> p (a b)")

    t_qkv = dram("t_qkv", [3, P, TOK])
    t_sza, t_y = dram("t_silu_za", [FT, P, TOK]), dram("t_y", [FT, P, TOK])
    t_sga, t_sgb = dram("t_sig_ga", [KT, P, TOK]), dram("t_sig_gb", [KT, P, TOK])
    t_oz, t_m = dram("t_oz", [HEADS, P, SEQ]), dram("t_merged", [KT, P, TOK])
    t_qs = dram("t_q_new", [NEW, WIDTH])

    c = Carve(work)
    xin = [c.take(D_MODEL) for _ in range(2)]
    xsq, gb_bc = c.take(D_MODEL), c.take(D_MODEL)
    tp = c.take(24 * 64, 64)

    c = Carve(work)
    uT, xy = c.take(TOK), c.take(TOK)
    Ug = c.take(8 * NCH).rearrange("p (g j) -> p g j", g=8)
    m_flat = c.take(1024)
    M1 = m_flat[:, 0:512].rearrange("p (g q) -> p g q", g=HG)
    M2 = m_flat[:, 512:1024].rearrange("p (g q) -> p g q", g=HG)
    Kt = m_flat[0:GC, 0:HG * 15 * GC].rearrange("p (g q) -> p g q", g=HG)
    T1, T2 = m_flat[:, 0:512], m_flat[:, 512:1024]
    N1 = c.take(HG * 9 * GC).rearrange("p (g q) -> p g q", g=HG)
    N2 = c.take(HG * 9 * GC).rearrange("p (g q) -> p g q", g=HG)
    Er = c.take(512).rearrange("p (g j) -> p g j", g=HG)
    Ei = c.take(512).rearrange("p (g j) -> p g j", g=HG)
    B1T = c.take(512).rearrange("p (g s) -> p g s", g=HG)
    B2T = c.take(512).rearrange("p (g s) -> p g s", g=HG)
    Toep = c.take(512).rearrange("p (g q) -> p g q", g=HG)
    v_flat = c.take(2 * HG * (NCH + 1))
    V1 = v_flat[:, 0:516].rearrange("p (g j) -> p g j", g=HG)
    V2 = v_flat[:, 516:1032].rearrange("p (g j) -> p g j", g=HG)
    PT = [v_flat[:, 256 * n:256 * n + 256] for n in range(4)]
    CR = c.take(P, 64)
    SR = c.take(HG * P, NEW).rearrange("p (g s) -> p g s", g=HG)
    SO = SR
    Bc, Bm = c.take(HG * GC), c.take(HG * GC)
    BcX, BmX = Bc.rearrange("p (g c) -> p g c", g=HG), Bm.rearrange("p (g c) -> p g c", g=HG)
    Us = c.take(8 * NEW, GC).rearrange("p (g b) -> p g b", g=8)
    h12 = c.take(2 * HG * NEW).rearrange("p (f g b) -> p f g b", f=2, g=HG)
    hA = c.take(HG * NEW).rearrange("p (g b) -> p g b", g=HG)
    hn = c.take(HG * NEW).rearrange("p (g b) -> p g b", g=HG)
    ysT = c.take(P, NEW)
    fs = c.take(2 * P, HG)
    fo = c.take(P, HG)
    pw = c.take(12 * HG)

    c = Carve(work)
    qT, kT, vT = c.take(TOK), c.take(TOK), c.take(TOK)
    wT = vT[:, 0:SEQ]
    vtok = c.take(SEQ)
    zb = [c.take(SEQ) for _ in range(2)]
    ktok = zb[1]
    lk, rl = c.take(SEQ), c.take(SEQ)
    szb = c.take(TOK)
    smp = c.take(3 * P, NEW)

    c = Carve(work)
    sz = [c.take(TOK) for _ in range(2)]
    ysum = c.take(TOK)
    kv_flat = c.take(2 * N_PAGES * WIDTH)
    kv = [kv_flat[:, b * 2 * WIDTH:(b + 1) * 2 * WIDTH] for b in range(2)]
    qbc = [c.take(WIDTH) for _ in range(2)]
    Zs = c.take(2 * 64)
    wsT = c.take(2 * 64)
    s_z, s_l, s_r = c.take(256, 64), c.take(256, 64), c.take(256, 64)
    ozs = c.take(HEADS * NEW)
    yin = [kv_flat[:, n * TOK:(n + 1) * TOK] for n in range(2)]
    ozin = [kv_flat[:, n * SEQ:(n + 1) * SEQ] for n in range(4)]

    c = Carve(work)
    ga, gb = [c.take(TOK) for _ in range(2)], [c.take(TOK) for _ in range(2)]
    MI = 6
    m_in = [c.take(TOK) for _ in range(MI)]

    c = Carve(work)
    h = c.take(4 * D_MODEL).rearrange("p (b n) -> p b n", b=4)
    nf = c.take(D_MODEL)

    raw_loaded = [sem("raw_loaded0"), sem("raw_loaded1")]
    hi_ready, lo_ready, chunk_used = sem("hi_ready"), sem("lo_ready"), sem("chunk_used")
    stage_ready = [sem("stage_ready0"), sem("stage_ready1")]
    stage_sent = [sem("stage_sent0"), sem("stage_sent1")]
    consts_ready, consts_in = sem("consts_ready"), sem("consts_in")
    act_chain, pool_consts, us_mm, us_ready, br_a, br_b, h_rstd, h_scaled, tp_ready = [sem(s) for s in
        ("act_chain", "pool_consts", "s5_us_mm", "s5_us_ready", "branch_a_used", "branch_b_used", "h_rstd", "h_scaled", "tables_made")]
    x_in = [sem("x_in0"), sem("x_in1")]
    x_sq, x_var, x_std, x_scaled, x_tr, x_hi, x_lo = [sem(s) for s in
        ("x_sq", "x_var", "x_std", "x_scaled", "x_transposed", "x_hi", "x_lo")]
    dve_chain, pool_chain = sem("dve_chain"), sem("pool_chain")
    par_in, par_t, tab_ready = sem("param_in"), sem("param_T"), sem("tables_ready")
    gate_exp, u_ready = sem("gate_exp"), sem("u_ready")
    s5_in, a_mm, seeded, m_ready, n_ready, e_ready, ha_ready = [sem(s) for s in
        ("s5_in", "s5_seed_mm", "s5_seeded", "s5_m_ready", "s5_n_ready", "s5_e_ready", "s5_ha_ready")]
    b_mm, bt_ready, k_mm, kt_ready, kt_pad, toep_in = [sem(s) for s in
        ("s5_b_mm", "s5_bt_ready", "s5_k_mm", "s5_kt_ready", "s5_kt_pad", "s5_toep_in")]
    xj_mm, xj_ready, ug_mm, ug_ready, pq_mm, v_ready, y_mm, yj_ready, fin_copied, fin_ready = [sem(s) for s in
        ("s5_xj_mm", "s5_xj_ready", "s5_ug_mm", "s5_ug_ready", "s5_pq_mm", "s5_v_ready", "s5_y_mm",
         "s5_yj_ready", "s5_fin_copied", "s5_fin_ready")]
    hn_ready, ys_mm, ys_ready, yt_mm, yt_ready, y_sent, st_sent = [sem(s) for s in
        ("s5_hn_ready", "s5_ys_mm", "s5_ys_ready", "s5_yt_mm", "s5_yt_ready", "s5_y_sent", "s5_state_sent")]
    at_in, v_tr, vtok_ready, k_tr, ktok_ready, new_tr, new_ready, kv_sent = [sem(s) for s in
        ("attn_in", "v_tr", "vtok_ready", "k_tr", "ktok_ready", "new_tr", "new_ready", "kv_sent")]
    sc_mm, z_ready, lr_ready, l_ready, arg_ready, w_ready, w_tr, wt_ready, pv_mm, oz_ready, oz_sent, szb_ready = [sem(s) for s in
        ("score_mm", "z_ready", "lr_ready", "log_ready", "arg_ready", "w_ready", "w_tr", "wt_ready", "pv_mm", "oz_ready",
         "oz_sent", "szb_ready")]
    xa_ready, xb_ready = sem("act_hi_ready"), sem("act_lo_ready")
    y_in = [sem("y_in0"), sem("y_in1")]
    gelu_done, sz_in, y2_ready = sem("gelu_done"), [sem("sz_in0"), sem("sz_in1")], sem("y2_ready")
    pg_in, pg_k, pg_v, q_in = sem("pages_in"), [sem("page_k0"), sem("page_k1")], [sem("page_v0"), sem("page_v1")], [sem("q_in0"), sem("q_in1")]
    kq_done, zs_part, zs_tr, slr_ready, sl_ready, sarg_ready, sw_ready, sw_tr, swt_ready, spv_mm, ozs_ready = [sem(s) for s in
        ("kq_done", "zs_part", "zs_tr", "slr_ready", "slog_ready", "sarg_ready", "sw_ready", "sw_tr", "swt_ready",
         "spv_mm", "ozs_ready")]
    oz_in = [sem(f"oz_in{n}") for n in range(4)]
    g_in = [sem("gates_in0"), sem("gates_in1")]
    m_in_s = [sem(f"merged_in{n}") for n in range(MI)]
    x_res, nf_in, h_std, h_norm, y_out = [sem(s) for s in ("x_res", "norm_f_in", "h_std", "h_norm", "y_out")]
    o_ready, o_tr, o_added = [[sem(f"{n}{s}") for s in range(2)] for n in ("out_evacuated", "out_transposed", "out_added")]
    h_var, osm_tr = sem("h_var"), sem("out_new_tr")
    glu_n, br_n = sem("glu_exp"), sem("merged_ready")

    GLU0 = FT * CHUNKS
    BR0 = GLU0 + FT
    OUT0 = BR0 + 2 * KT

    block = stack.enter_context(nc.Block())

    rawf = [r[:, :, :] for r in raw]
    xres_v = x_prompt[0]

    def f32(ap):
        return ap.bitcast(F32)

    def acc_v(s, n=NC, banks=NB):
        return acc[s][:, 0:banks, 0:n]

    def tok3(ap):
        return ap.rearrange("p (b n) -> p b n", b=NB)

    @block.sync
    def _(sp):
        def load_chunk(src, k0, col, m, b):
            sp.dma_start(rawf[b], src[k0 * P:(k0 + CK) * P, col].rearrange("(k p) n -> p k n", p=P)).then_inc(raw_loaded[b], 16)

        sp.dma_start(gb_bc, norm_g[0:1, :].to_broadcast([P, D_MODEL])).then_inc(consts_in, 16)
        for b in range(2):
            sp.dma_start(xin[b], x_prompt[0, b * P:(b + 1) * P, :]).then_inc(x_in[b], 16)
        sp.dma_start(tp[:, 0:64], A_re[0]).then_inc(par_in, 16)
        sp.dma_start(tp[:, 64:128], A_im[0]).then_inc(par_in, 16)
        sp.dma_start(tp[:, 128:129], log_dt.rearrange("a g -> g a")).then_inc(par_in, 16)
        sp.dma_start(dcol[:, :], Dw[0].rearrange("(f p) -> p f", p=P), allow_slow_non_contiguous=True).then_inc(consts_in, 16)
        sp.dma_start(nglub[:, :], glu_b[0].rearrange("(f p) -> p f", p=P), allow_slow_non_contiguous=True).then_inc(consts_in, 16)
        sp.dma_start(bias_all[:, :], sb_bias[0:1, :].to_broadcast([P, HEADS])).then_inc(consts_in, 16)
        for b in range(NEW):
            sp.dma_start(bias64[b * HEADS:(b + 1) * HEADS, :], sb_bias.rearrange("a h -> h a")).then_inc(consts_in, 16)
        sp.dma_start(pages[:, :], page_table.rearrange("b n -> (b n)").unsqueeze(0)).then_inc(pg_in, 16)
        with sp.Fori(0, 3) as r:
            for b in range(2):
                sp.wait_ge(x_tr, 8 * r + 4 * b + 4)
                sp.dma_start(xin[b], x_prompt[0, bass.ds(r * (2 * P) + (2 + b) * P, P), :]).then_inc(x_in[b], 16)
        sp.wait_ge(x_tr, 28)
        sp.dma_start(xin[0][0:NEW, :], x_sample.rearrange("b o n -> (b o) n")).then_inc(x_in[0], 16)
        for b in range(2):
            load_chunk(w_in[0], b * CK, slice(0, P), 0, b)
        sp.wait_ge(x_tr, 36)
        sp.wait_ge(par_t, 1)

        def phase_a(i, last):
            if not last:
                for scale in (48, 64, 80, 128, 256, 512, 1024):
                    sp.lower_val(i * scale)
                sp.lower_val(i * P * 4)
                sp.lower_val(i * 128 + 64)
                sp.lower_val(i * 64 + 32)
                sp.lower_val(i * 64 + 48)
                sp.lower_val((i + 1) * 128)
                sp.lower_val((i + 1) * 16)
                sp.lower_val((i + 1) * 128 * 4)

            def ahead(cn):
                sp.wait_ge(lo_ready, i * CHUNKS + cn + 1)
                b = cn % 2
                if cn + 2 < CHUNKS:
                    t = (cn + 2) // 2
                    load_chunk(w_in[0], b * CK, bass.ds(weight_column(t, i), P), 0, b)
                elif not last:
                    load_chunk(w_in[0], b * CK, bass.ds(weight_column(U, i + 1), P), 0, b)
                else:
                    load_chunk(glu_w[0], 0, slice(b * P, (b + 1) * P), 0, b)

            def send(t):
                n = (ZA, GB0, Q, K, V, GB1, GA0, GA1).index(t)
                s, m = n % 2, n // 2
                sp.wait_ge(stage_ready[s], i * 4 + m + 1)
                if t == Q:
                    sp.wait_ge(at_in, i * 48)
                dst = {ZA: lambda: t_sza[bass.ds(i, 1)], Q: lambda: t_qkv[0:1], K: lambda: t_qkv[1:2],
                       V: lambda: t_qkv[2:3], GB0: lambda: t_sgb[bass.ds(2 * i, 1)],
                       GB1: lambda: t_sgb[bass.ds(2 * i + 1, 1)], GA0: lambda: t_sga[bass.ds(2 * i, 1)],
                       GA1: lambda: t_sga[bass.ds(2 * i + 1, 1)]}[t]()
                sp.dma_start(dst.rearrange("a p n -> (a p) n"), stage[s][:, :]).then_inc(stage_sent[s], 16)

            def s5_params(hf):
                if hf == 0:
                    sp.wait_ge(oz_sent, i * 16)
                    sp.wait_ge(kv_sent, i * 80)
                else:
                    sp.wait_ge(ha_ready, i * 2 + 1)
                    sp.wait_ge(seeded, i * 2 + 1)
                    sp.wait_ge(st_sent, i * 128 + 64)
                g0 = i * (2 * HG) + hf * HG
                Bv = [x[0, bass.ds(g0, HG)].rearrange("g n c -> n g c") for x in (B_re, B_im)]
                Cv = [x[0, bass.ds(g0, HG)].rearrange("g c n -> (g c) n") for x in (C_re, C_im)]
                Sv = [x[0, :, bass.ds(g0, HG), :] for x in (st_re, st_im)]
                sp.dma_start(BcX[0:64], Bv[0]).then_inc(s5_in, 16)
                sp.dma_start(BcX[64:128], Bv[1]).then_inc(s5_in, 16)
                sp.dma_start(BmX[0:64], Bv[1]).then_inc(s5_in, 16)
                sp.dma_start(BmX[64:128], Bv[0]).then_inc(s5_in, 16)
                sp.dma_start(CR[:, 0:64], Cv[0]).then_inc(s5_in, 16)
                sp.dma_start(CR[:, 64:128], Cv[1]).then_inc(s5_in, 16)
                sp.dma_start(SR[:, :, 0:64], Sv[0]).then_inc(s5_in, 16)
                sp.dma_start(SR[:, :, 64:128], Sv[1]).then_inc(s5_in, 16)

            def toeplitz(hf):
                sp.wait_ge(kt_ready, i * 2 + hf + 1)
                sp.wait_ge(kt_pad, i * 2 + hf + 1)
                for tau in range(CH):
                    sp.dma_start(Toep[tau * GC:(tau + 1) * GC], Kt[:, :, tau * GC:(tau + CH) * GC]).then_inc(toep_in, 16)

            def s5_states(hf):
                g0 = i * (2 * HG) + hf * HG
                sp.wait_ge(fin_ready, i * 2 + hf + 1)
                for part, out in ((0, re_prompt), (1, im_prompt)):
                    sp.dma_start(out[0, 0, bass.ds(g0, HG), :], fo[:, part * 64:(part + 1) * 64]).then_inc(st_sent, 16)
                sp.wait_ge(ys_ready, i * 2 + hf + 1)
                for part, out in ((0, re_sample), (1, im_sample)):
                    sp.dma_start(out[0, :, bass.ds(g0, HG), :], SO[:, :, part * 64:(part + 1) * 64]).then_inc(st_sent, 16)

            def s5_out():
                sp.wait_ge(yt_ready, 2 * i + 2)
                sp.dma_start(t_y[bass.ds(i, 1)].rearrange("a p n -> (a p) n"), xy).then_inc(y_sent, 16)

            def attn_load():
                sp.wait_ge(y_sent, (i + 1) * 16)
                sp.wait_ge(st_sent, (i + 1) * 128)
                sp.wait_ge(stage_sent[0], i * 64 + 48)
                sp.wait_ge(stage_sent[1], i * 64 + 32)
                for n, dst in enumerate((qT, kT, vT)):
                    sp.dma_start(dst, t_qkv[n]).then_inc(at_in, 16)

            def kv_out():
                for ready, src, out in ((vtok_ready, vtok, v_prompt), (ktok_ready, ktok, k_prompt)):
                    sp.wait_ge(ready, i + 1)
                    sp.dma_start(out[0, 0].rearrange("(b p) h d -> p b h d", p=P)[:, :, bass.ds(i, 1), :].rearrange("p b h d -> p b (h d)"),
                                 src.rearrange("p (b d) -> p b d", b=8)).then_inc(kv_sent, 16)
                sp.wait_ge(new_ready, i + 1)
                sp.dma_start(t_qs[:, bass.ds(i * P, P)], smp[:, 0:P]).then_inc(kv_sent, 16)
                for n, out in ((1, k_sample), (2, v_sample)):
                    sp.dma_start(out[0, :, 0, bass.ds(i, 1), :].rearrange("b h d -> b (h d)"), smp[:, n * P:(n + 1) * P]).then_inc(kv_sent, 16)

            def oz_out():
                sp.wait_ge(oz_ready, i * 8 + 8)
                sp.dma_start(t_oz[bass.ds(i, 1)].rearrange("a p n -> (a p) n"), szb[:, 0:SEQ]).then_inc(oz_sent, 16)

            for cn in range(CHUNKS):
                ahead(cn)
                if cn % 2 == 1 and cn > 1 and cn // 2 - 1 not in (U, ZB):
                    send(cn // 2 - 1)
                if cn == 0:
                    s5_params(0)
                if cn == 4:
                    toeplitz(0)
                if cn == 6:
                    s5_states(0)
                    s5_params(1)
                if cn == 9:
                    toeplitz(1)
                if cn == 11:
                    s5_states(1)
                    s5_out()
                if cn == 13:
                    attn_load()
                if cn == 15:
                    kv_out()
            oz_out()
            send(GA1)

        with sp.Fori(0, FT - 1) as i:
            phase_a(i, False)
        phase_a(FT - 1, True)

        sp.wait_ge(oz_sent, FT * 16)
        sp.wait_ge(kv_sent, FT * 80)
        sp.wait_ge(y_sent, FT * 16)
        for s in range(2):
            sp.wait_ge(stage_sent[s], FT * 64)
        for t in range(FT):
            b = t % 2
            if t >= 2:
                sp.wait_ge(xb_ready, t - 1)
                sp.wait_ge(xa_ready, t - 1)
            sp.dma_start(yin[b], t_y[t]).then_inc(y_in[b], 16)
        for b in range(2):
            sp.dma_start(sz[b], t_sza[b]).then_inc(sz_in[b], 16)
        sp.wait_ge(pg_in, 16)
        sp.wait_ge(xb_ready, FT)
        sp.wait_ge(xa_ready, FT)

        def load_pages(cache, b, sems):
            for n in range(N_PAGES):
                page = sp.value_load(pages[0:1, b * N_PAGES + n:b * N_PAGES + n + 1], min_val=0,
                                     max_val=cache.shape[1] - 1)
                sp.dma_start(kv[b % 2][:, n * WIDTH:(n + 1) * WIDTH],
                             cache[0, bass.ds(page, 1)].rearrange("a t h d -> (a t) (h d)")).then_inc(sems[b % 2], 16)

        for f in range(FT):
            sp.wait_ge(lo_ready, GLU0 + f + 1)
            b = f % 2
            if f + 2 < FT:
                load_chunk(glu_w[0], 0, slice((f + 2) * P, (f + 3) * P), 0, b)
            else:
                load_chunk((w_a, w_b)[b][0], 0, slice(0, P), 0, b)
            if f >= 1 and f + 1 < FT:
                sp.wait_ge(y2_ready, f)
                sp.dma_start(sz[(f + 1) % 2], t_sza[f + 1]).then_inc(sz_in[(f + 1) % 2], 16)
            if f < 4:
                for bb in (2 * f, 2 * f + 1):
                    if bb >= 2:
                        sp.wait_ge(zs_part, bb - 1)
                    load_pages(cache_k, bb, pg_k)
                    sp.dma_start(qbc[bb % 2], t_qs[bb:bb + 1, :].to_broadcast([P, WIDTH])).then_inc(q_in[bb % 2], 16)
            else:
                for bb in (2 * (f - 4), 2 * (f - 4) + 1):
                    if bb < 2:
                        sp.wait_ge(zs_part, 7 + bb)
                    else:
                        sp.wait_ge(spv_mm, bb - 1)
                    load_pages(cache_v, bb, pg_v)
        sp.wait_ge(spv_mm, NEW)
        for t in range(HEADS):
            if t >= 4:
                sp.wait_ge(xb_ready, FT + FT + t - 3)
            sp.dma_start(ozin[t % 4], t_oz[t]).then_inc(oz_in[t % 4], 16)
        sp.wait_ge(xb_ready, 3 * FT)
        sp.wait_ge(xa_ready, 3 * FT)
        sp.wait_ge(y2_ready, FT)
        for b in range(2):
            sp.dma_start(ga[b], t_sga[b]).then_inc(g_in[b], 16)
            sp.dma_start(gb[b], t_sgb[b]).then_inc(g_in[b], 16)

        def branch(j, tail):
            for b2 in range(2):
                for b in range(2):
                    sp.wait_ge(lo_ready, BR0 + 4 * j + 2 * b2 + b + 1)
                    if not (tail and b2 == 1):
                        load_chunk((w_a, w_b)[b][0], 0, bass.ds((2 * j + b2 + 1) * P, P), 0, b)
                    else:
                        load_chunk(w_out[0], b * CK, slice(0, P), 0, b)
            for b2 in range(2):
                sp.wait_ge(br_n, 2 * j + b2 + 1)
                sp.dma_start(t_m[bass.ds(2 * j + b2, 1)].rearrange("a p n -> (a p) n"), stage[b2][:, :]).then_inc(stage_sent[b2], 16)
                if not tail:
                    sp.dma_start(ga[b2], t_sga[bass.ds(2 * j + 2 + b2, 1)].rearrange("a p n -> (a p) n")).then_inc(g_in[b2], 16)
                    sp.dma_start(gb[b2], t_sgb[bass.ds(2 * j + 2 + b2, 1)].rearrange("a p n -> (a p) n")).then_inc(g_in[b2], 16)

        with sp.Fori(0, KT // 2 - 1) as j:
            branch(j, False)
        branch(KT // 2 - 1, True)
        for s in range(2):
            sp.wait_ge(stage_sent[s], FT * 64 + KT // 2 * 16)
        for t in range(KT):
            if t >= MI:
                sp.wait_ge(xb_ready, 3 * FT + t - MI + 1)
                sp.wait_ge(xa_ready, 3 * FT + t - MI + 1)
            sp.dma_start(m_in[t % MI], t_m[t]).then_inc(m_in_s[t % MI], 16)
        sp.wait_ge(xb_ready, 3 * FT + KT)
        sp.wait_ge(xa_ready, 3 * FT + KT)
        sp.dma_start(nf, norm_f.unsqueeze(0).to_broadcast([P, D_MODEL])).then_inc(nf_in, 16)

        def out_weights(base, j, wrap):
            for b2 in range(2):
                for b in range(2):
                    sp.wait_ge(lo_ready, base + 4 * j + 2 * b2 + b + 1)
                    if wrap is None or b2 == 0:
                        load_chunk(w_out[0], b * CK, bass.ds((2 * j + b2 + 1) * P, P), 0, b)
                    elif wrap:
                        load_chunk(w_out[0], b * CK, slice(0, P), 0, b)

        for half in range(2):
            for blk in range(4):
                if half == 1:
                    sp.wait_ge(y_out, 64)
                sp.dma_start(h[:, blk, :], x_prompt[0, (4 * half + blk) * P:(4 * half + blk + 1) * P, :]).then_inc(x_res, 16)
            with sp.Fori(0, KT // 2 - 1) as j:
                out_weights(OUT0 + 32 * half, j, None)
            out_weights(OUT0 + 32 * half, KT // 2 - 1, half == 0)
            for blk in range(4):
                sp.wait_ge(h_norm, 4 * half + blk + 1)
                sp.dma_start(y_prompt[0, (4 * half + blk) * P:(4 * half + blk + 1) * P, :], h[:, blk, :]).then_inc(y_out, 16)
        sp.wait_ge(y_out, 8 * 16)
        sp.dma_start(h[0:NEW, 0, :], x_sample.rearrange("b o n -> (b o) n")).then_inc(x_res, 16)
        sp.wait_ge(h_norm, 9)
        sp.dma_start(y_sample.rearrange("b o n -> (b o) n"), h[0:NEW, 0, :]).then_inc(y_out, 16)
        sp.wait_ge(y_out, 9 * 16)
        sp.wait_ge(kv_sent, FT * 80)
        sp.wait_ge(st_sent, FT * 128)

    SEED, BT, KM, PQ, YM, YS = (3, 22), (8, 30), (13, 32), (15, 34), (18, 37), (19, 38)
    XJ, UG, US, YT = 10, 11, 12, 40
    VT, KTR, NTR, SC0 = 52, 53, 54, 55
    SC = tuple(SC0 if q == 0 else 56 + 3 * (q - 1) for q in range(8))
    WT = tuple(57 + 3 * q for q in range(8))
    PV = tuple(58 + 3 * q if q < 7 else 79 for q in range(8))
    STAGED = (ZA, GB0, Q, K, V, GB1, GA0, GA1)
    GATES = (ZA, GB0, ZB, GB1, GA0, GA1)

    def stage_of(t):
        n = STAGED.index(t)
        return n % 2, n // 2

    @block.scalar
    def _(act):
        def norm_block(b, r16, done, rows, dst):
            act.wait_ge(x_in[b], r16)
            act.wait_ge(x_scaled, done)
            nc.scalar.activation(xsq[0:rows, :], xin[b][0:rows, :], ACT.Square, accum_out=stat[0:rows, 0:1]).then_inc(x_sq, 1)
            act.wait_ge(x_var, done + 1)
            nc.scalar.activation(stat[0:rows, 2:3], stat[0:rows, 1:2], ACT.Sqrt).then_inc(x_std, 1)
            for q in range(4):
                act.wait_ge(x_tr, done * 4 + q + 1)
                src = acc[q % 2][:, q // 2, :].rearrange("p (k t) -> p k t", k=4)[:, :, 0:rows]
                nc.scalar.copy(XH[:, 4 * q:4 * q + 4, dst], src).then_inc(x_hi, 1)

        act.wait_ge(pool_consts, 1)
        nc.scalar.copy(stat[:, 7:8], zero1[:, :]).then_inc(gate_exp, 1)
        with act.Fori(0, 4) as r:
            for b in range(2):
                norm_block(b, 16 * r + 16, 2 * r + b, P, bass.ds(r * (2 * P) + b * P, P))
        norm_block(0, 80, 8, NEW, slice(SEQ, TOK))
        act.wait_ge(raw_loaded[0], 16)
        nc.scalar.copy(hi[0][:, :, :], raw[0][:, :, :]).then_inc(hi_ready, 1)
        act.wait_ge(par_t, 1)
        nc.scalar.copy(tab[:, :, :], side[:, 0, 0:7 * GROUPS].rearrange("p (a g) -> p a g", a=7)).then_inc(tab_ready, 1)

        def evacuate(i, t):
            act.wait_ge(chunk_used, i * CHUNKS + 2 * (t + 1))
            if t == U:
                act.wait_ge(s5_in, i * 256 + 128)
                nc.scalar.copy(tok3(uT), acc_v(0)).then_inc(u_ready, 1)
                return
            if t == ZB:
                act.wait_ge(at_in, i * 48 + 48)
                nc.scalar.activation(tok3(szb), acc_v(t % 2), ACT.Exp, scale=-1.0).then_inc(gate_exp, 1)
                return
            s, m = stage_of(t)
            act.wait_ge(stage_sent[s], i * 64 + 16 * m)
            if t in (Q, K, V):
                nc.scalar.copy(tok3(stage[s][:, :]), acc_v(t % 2)).then_inc(stage_ready[s], 1)
            else:
                nc.scalar.activation(tok3(stage[s][:, :]), acc_v(t % 2), ACT.Exp, scale=-1.0).then_inc(gate_exp, 1)

        def split_hi(b, loaded, used):
            act.wait_ge(raw_loaded[b], loaded)
            act.wait_ge(chunk_used, used)
            nc.scalar.copy(hi[b][:, :, :], raw[b][:, :, :]).then_inc(hi_ready, 1)

        with act.Fori(0, FT) as i:
            for p in range(PTS):
                if p % 4 == 0:
                    cn = p // 4 + 1
                    split_hi(cn % 2, i * (CHUNKS * 8) + 16 * (cn // 2) + 16, i * CHUNKS + cn - 1)
                if p % 8 == 0 and p:
                    evacuate(i, p // 8 - 1)
                for hf in range(2):
                    if p == SEED[hf]:
                        act.wait_ge(a_mm, 2 * i + hf + 1)
                        nc.scalar.copy(N1[:, :, 0:GC], side[:, 0, 0:64].rearrange("p (g c) -> p g c", g=HG))
                        nc.scalar.copy(N2[:, :, 0:GC], side[:, 0, 64:128].rearrange("p (g c) -> p g c", g=HG))
                        nc.scalar.copy(h12, side[:, 0, 128:192].rearrange("p (f g b) -> p f g b", f=2, g=HG)).then_inc(seeded, 1)
                    if p == BT[hf]:
                        act.wait_ge(b_mm, 2 * i + hf + 1)
                        nc.scalar.copy(B1T, side[:, 0, :].rearrange("p (g s) -> p g s", g=HG))
                        nc.scalar.copy(B2T, side[:, 1, :].rearrange("p (g s) -> p g s", g=HG)).then_inc(bt_ready, 1)
                    if p == KM[hf]:
                        act.wait_ge(k_mm, 2 * i + hf + 1)
                        nc.scalar.copy(Kt[:, :, 7 * GC:15 * GC], side[0:GC, 0, :].rearrange("p (g q) -> p g q", g=HG)).then_inc(kt_ready, 1)
                    if p == YM[hf]:
                        act.wait_ge(y_mm, 2 * i + hf + 1)
                        nc.scalar.copy(fs, side[0:HG, 1, 0:2 * P]).then_inc(fin_copied, 1)
                        for g in range(HG):
                            dst = xy[:, 0:SEQ].rearrange("p (t f) -> p t f", t=CH)[:, :, hf * 64 + g * GC:hf * 64 + (g + 1) * GC]
                            last = nc.scalar.copy(dst, side[:, 0, g * P:(g + 1) * P].rearrange("p (t c) -> p t c", t=CH))
                        last.then_inc(yj_ready, 1)
                    if p == YS[hf]:
                        act.wait_ge(ys_mm, 2 * i + hf + 1)
                        nc.scalar.copy(ysT[:, hf * 64:(hf + 1) * 64], side[0:NEW, 1, 0:64])
                        nc.scalar.copy(SO, side[0:NEW, 0, :].rearrange("p (g s) -> p g s", g=HG)).then_inc(ys_ready, 1)
                if p == XJ:
                    act.wait_ge(xj_mm, i + 1)
                    for tau in range(CH):
                        last = nc.scalar.copy(xy[:, 0:SEQ].rearrange("p (g t c) -> p t g c", g=8, t=CH)[:, tau],
                                              side_flat[:, tau * P:(tau + 1) * P].rearrange("p (g c) -> p g c", g=8))
                    last.then_inc(xj_ready, 1)
                if p == UG:
                    act.wait_ge(ug_mm, i + 1)
                    nc.scalar.copy(Ug, side_flat.rearrange("p (g j) -> p g j", g=8)).then_inc(ug_ready, 1)
                if p == US:
                    act.wait_ge(us_mm, i + 1)
                    nc.scalar.copy(Us, side[0:GC, 0, 0:64].rearrange("p (g b) -> p g b", g=8)).then_inc(us_ready, 1)
                if p == VT:
                    act.wait_ge(v_tr, i + 1)
                    nc.scalar.copy(vtok, side_flat).then_inc(vtok_ready, 1)
                if p == KTR:
                    act.wait_ge(k_tr, i + 1)
                    nc.scalar.copy(ktok, side_flat).then_inc(ktok_ready, 1)
                if p == NTR:
                    act.wait_ge(new_tr, i + 1)
                    nc.scalar.copy(smp, side[0:NEW, 0, 0:3 * P]).then_inc(new_ready, 1)
                for qb in range(8):
                    w = P * (qb + 1)
                    if p == WT[qb] - 1:
                        act.wait_ge(arg_ready, 8 * i + qb + 1)
                        nc.scalar.activation(zb[qb % 2][:, 0:w], zb[qb % 2][:, 0:w], ACT.Exp).then_inc(w_ready, 1)
                    if p == WT[qb]:
                        act.wait_ge(w_tr, 8 * i + qb + 1)
                        nc.scalar.copy(wT[:, 0:w], side_flat[:, 0:w]).then_inc(wt_ready, 1)
                for qb in range(8):
                    w = P * (qb + 1)
                    if p == SC[qb]:
                        act.wait_ge(lr_ready, 8 * i + qb + 1)
                        nc.scalar.activation(lk[:, 0:w], lk[:, 0:w], ACT.Exp).then_inc(act_chain, 1)
                        act.wait_ge(act_chain, 8 * i + qb + 1)
                        nc.scalar.activation(lk[:, 0:w], lk[:, 0:w], ACT.Ln, bias=1.0).then_inc(l_ready, 1)
            evacuate(i, GA1)


        act.wait_ge(chunk_used, GLU0)
        for t in range(FT):
            act.wait_ge(y_in[t % 2], 16 * (t // 2 + 1))
            nc.scalar.activation(yin[t % 2], yin[t % 2], ACT.Gelu).then_inc(gelu_done, 1)
            act.wait_ge(gelu_done, t + 1)
            nc.scalar.copy(XH[:, t, :], yin[t % 2]).then_inc(xa_ready, 1)
        for f in range(FT):
            split_hi((f + 1) % 2, 16 * ((GLU0 + f + 1) // 2 + 1), GLU0 + f)
            act.wait_ge(chunk_used, GLU0 + f + 1)
            if f < 2:
                act.wait_ge(stage_sent[f], FT * 64)
            else:
                act.wait_ge(xb_ready, FT + f - 1)
            nc.scalar.activation(tok3(stage[f % 2][:, :]), acc_v(f % 2), ACT.Exp, bias=nglub[:, f:f + 1], scale=-1.0).then_inc(glu_n, 1)
            act.wait_ge(y2_ready, f + 1)
            nc.scalar.copy(XH[:, FT + f, :], stage[f % 2][:, :]).then_inc(xa_ready, 1)
            if f == 4:
                act.wait_ge(slr_ready, 1)
                nc.scalar.activation(s_l, s_l, ACT.Exp).then_inc(sl_ready, 1)
                act.wait_ge(sl_ready, 1)
                nc.scalar.activation(s_l, s_l, ACT.Ln, bias=1.0).then_inc(sl_ready, 1)
                act.wait_ge(sarg_ready, 1)
                nc.scalar.activation(s_z, s_z, ACT.Exp).then_inc(sw_ready, 1)
            if f == 5:
                act.wait_ge(sw_tr, 1)
                nc.scalar.copy(wsT, side[:, 0, 0:P]).then_inc(swt_ready, 1)
        act.wait_ge(chunk_used, BR0)
        act.wait_ge(y2_ready, FT)
        for t in range(HEADS):
            act.wait_ge(oz_in[t % 4], 16 * (t // 4 + 1))
            nc.scalar.copy(XH[:, t, 0:SEQ], ozin[t % 4])
            if t == 0:
                act.wait_ge(ozs_ready, 1)
            nc.scalar.copy(XH[:, t, SEQ:TOK], ozs[:, t * NEW:(t + 1) * NEW]).then_inc(xa_ready, 1)
        with act.Fori(0, KT // 2) as j:
            for n in range(4):
                split_hi((n + 1) % 2, j * 32 + 16 * (BR0 // 2 + (n + 1) // 2 + 1), j * 4 + (BR0 + n))
        act.wait_ge(chunk_used, OUT0)
        for t in range(KT):
            act.wait_ge(m_in_s[t % MI], 16 * (t // MI + 1))
            nc.scalar.copy(XH[:, t, :], m_in[t % MI]).then_inc(xa_ready, 1)

        def out_tiles(half, j, last):
            for n in range(4):
                if not (last and n == 3):
                    split_hi((n + 1) % 2, j * 32 + 16 * (OUT0 // 2 + 16 * half + (n + 1) // 2 + 1), j * 4 + (OUT0 + 32 * half + n))
                if n % 2:
                    s = n // 2
                    act.wait_ge(chunk_used, j * 4 + (OUT0 + 32 * half + n + 1))
                    act.wait_ge(o_tr[s], j + 8 * half)
                    if half == 0:
                        nc.scalar.copy(stage[s][:, 0:512], acc[s][:, 0, :]).then_inc(o_ready[s], 1)
                    else:
                        nc.scalar.copy(outs_new[:, bass.ds(j * 2 + s, 1), :], acc[s][:, 1, 252:260].unsqueeze(1))
                        nc.scalar.copy(stage[s][:, 0:520].rearrange("p (a n) -> p a n", a=2), acc[s][:, 0:2, 0:260]).then_inc(o_ready[s], 1)

        def scale_rows(half):
            act.wait_ge(h_var, half + 1)
            nc.scalar.activation(stat[:, 2:6], hvar, ACT.Sqrt).then_inc(h_std, 1)
            act.wait_ge(h_rstd, half + 1)
            for blk in range(4):
                nc.scalar.mul(h[:, blk, :], h[:, blk, :], rstd4[:, blk:blk + 1]).then_inc(h_scaled, 1)

        with act.Fori(0, KT // 2) as j:
            out_tiles(0, j, False)
        scale_rows(0)
        with act.Fori(0, KT // 2 - 1) as j:
            out_tiles(1, j, False)
        out_tiles(1, KT // 2 - 1, True)
        scale_rows(1)
        act.wait_ge(h_var, 3)
        nc.scalar.activation(stat[0:NEW, 2:3], hvar[0:NEW, 0:1], ACT.Sqrt).then_inc(h_std, 1)
        act.wait_ge(h_rstd, 3)
        nc.scalar.mul(h[0:NEW, 0, :], h[0:NEW, 0, :], rstd4[0:NEW, 0:1]).then_inc(h_scaled, 1)

    @block.gpsimd
    def _(pool):
        nc.gpsimd.memset(zero1[:, :], 0.0).then_inc(pool_chain, 1)
        nc.gpsimd.memset(ident[:, :], 0.0).then_inc(pool_chain, 1)
        nc.gpsimd.memset(negid[:, :], 0.0).then_inc(pool_chain, 1)
        nc.gpsimd.memset(cmask[:, :], 0.0).then_inc(pool_chain, 1)
        pool.wait_ge(pool_chain, 4)
        nc.gpsimd.affine_select(out=ident[:, :], in_=ident[:, :], compare_op=ALU.not_equal, fill=1.0, base=0,
                                pattern=[[-1, P]], channel_multiplier=1)
        nc.gpsimd.affine_select(out=negid[:, :], in_=negid[:, :], compare_op=ALU.not_equal, fill=-1.0, base=0,
                                pattern=[[-1, 64]], channel_multiplier=1)
        nc.gpsimd.affine_select(out=cmask[:, :], in_=cmask[:, :], compare_op=ALU.is_gt, fill=NEG, base=0,
                                pattern=[[-1, P]], channel_multiplier=1).then_inc(pool_consts, 1)

        PER = 2 * POOL_HALF
        with pool.Fori(0, FT) as i:
            for hf in range(2):
                step = Chain(pool, pool_chain, i * PER + (4 + hf * POOL_HALF))
                pool.wait_ge(s5_in, i * 256 + 128 * (hf + 1))
                if hf == 0:
                    pool.wait_ge(tab_ready, 1)
                else:
                    pool.wait_ge(y_mm, 2 * i + 1)
                    pool.wait_ge(hn_ready, 2 * i + 1)
                pwv = pw.rearrange("p (a g) -> p a g", a=12)
                step(nc.gpsimd.tensor_copy(pwv[:, 0:7, :], tab[:, :, bass.ds(i * (2 * HG) + hf * HG, HG)]),
                     nc.gpsimd.memset(Er[:, :, 0:1], 1.0), nc.gpsimd.memset(Ei[:, :, 0:1], 0.0))
                step(nc.gpsimd.tensor_tensor(Bm[64:128, :], zero1[64:128, :].broadcast_to([64, HG * GC]), Bm[64:128, :], ALU.subtract))

                def wide(a, n):
                    return pwv[:, a, :].unsqueeze(2).broadcast_to([P, HG, n])

                def cmul(o1, o2, x1, x2, cr, ci, n, sign, done=None):
                    t = [q[:, 0:HG * n].rearrange("p (g n) -> p g n", g=HG) for q in PT]
                    step(nc.gpsimd.tensor_tensor(t[0], x1, wide(cr, n), ALU.mult),
                         nc.gpsimd.tensor_tensor(t[1], x2, wide(ci, n), ALU.mult),
                         nc.gpsimd.tensor_tensor(t[2], x2, wide(cr, n), ALU.mult),
                         nc.gpsimd.tensor_tensor(t[3], x1, wide(ci, n), ALU.mult))
                    first, second = (ALU.subtract, ALU.add) if sign > 0 else (ALU.add, ALU.subtract)
                    if done is None:
                        step(nc.gpsimd.tensor_tensor(o1, t[0], t[1], first),
                             nc.gpsimd.tensor_tensor(o2, t[2], t[3], second))
                    else:
                        step(nc.gpsimd.tensor_tensor(o1, t[0], t[1], first))
                        nc.gpsimd.tensor_tensor(o2, t[2], t[3], second).then_inc(done, 1)
                        pool.wait_ge(done, 2 * i + hf + 1)

                def square(cr, ci):
                    a, b = pwv[:, cr, :], pwv[:, ci, :]
                    step(nc.gpsimd.tensor_tensor(pwv[:, 7, :], a, a, ALU.mult),
                         nc.gpsimd.tensor_tensor(pwv[:, 8, :], b, b, ALU.mult),
                         nc.gpsimd.tensor_tensor(pwv[:, 9, :], a, b, ALU.mult))
                    step(nc.gpsimd.tensor_tensor(a, pwv[:, 7, :], pwv[:, 8, :], ALU.subtract),
                         nc.gpsimd.tensor_tensor(b, pwv[:, 9, :], pwv[:, 9, :], ALU.add))

                cmul(M1[:, :, 0:GC], M2[:, :, 0:GC], BcX, BmX, 2, 3, GC, 1)
                pool.wait_ge(seeded, 2 * i + hf + 1)
                tA = [q[:, 0:HG * NEW].rearrange("p (g b) -> p g b", g=HG) for q in PT]
                step(nc.gpsimd.tensor_tensor(tA[0], h12[:, 0], wide(0, NEW), ALU.mult),
                     nc.gpsimd.tensor_tensor(tA[1], h12[:, 1], wide(1, NEW), ALU.mult))
                nc.gpsimd.tensor_tensor(hA, tA[0], tA[1], ALU.subtract).then_inc(ha_ready, 1)
                pool.wait_ge(ha_ready, 2 * i + hf + 1)
                for n in (1, 2, 4):
                    w = n * GC
                    cmul(M1[:, :, w:2 * w], M2[:, :, w:2 * w], M1[:, :, 0:w], M2[:, :, 0:w], 0, 1, w, 1,
                         m_ready if n == 4 else None)
                    cmul(N1[:, :, w:2 * w], N2[:, :, w:2 * w], N1[:, :, 0:w], N2[:, :, 0:w], 0, 1, w, -1)
                    if n < 4:
                        square(0, 1)
                cmul(N1[:, :, 8 * GC:9 * GC], N2[:, :, 8 * GC:9 * GC], N1[:, :, 4 * GC:5 * GC], N2[:, :, 4 * GC:5 * GC], 0, 1, GC, -1,
                     n_ready)
                for k in range(7):
                    w = 1 << k
                    cmul(Er[:, :, w:2 * w], Ei[:, :, w:2 * w], Er[:, :, 0:w], Ei[:, :, 0:w], 4, 5, w, 1,
                         e_ready if k == 6 else None)
                    if k < 6:
                        square(4, 5)
                assert step.n == POOL_HALF, step.n
        for b in range(NEW):
            pool.wait_ge(pg_k[b % 2], 32 * (b // 2 + 1))
            pool.wait_ge(q_in[b % 2], 16 * (b // 2 + 1))
            kb = kv[b % 2].rearrange("p (a n) -> p a n", a=N_PAGES)
            nc.gpsimd.tensor_tensor(kb, kb, qbc[b % 2].unsqueeze(1).broadcast_to([P, N_PAGES, WIDTH]), ALU.mult).then_inc(kq_done, 1)
        pool.wait_ge(nf_in, 16)
        for n in range(8):
            pool.wait_ge(h_scaled, n + 1)
            nc.gpsimd.tensor_tensor(h[:, n % 4, :], h[:, n % 4, :], nf, ALU.mult).then_inc(h_norm, 1)
        pool.wait_ge(h_scaled, 9)
        nc.gpsimd.tensor_tensor(h[0:NEW, 0, :], h[0:NEW, 0, :], nf[0:NEW, :], ALU.mult).then_inc(h_norm, 1)

    @block.vector
    def _(dve):
        V = nc.vector
        step = Chain(dve, dve_chain)

        T = [tp[:, 64 * n:64 * n + 64] for n in range(24)]
        dve.wait_ge(par_in, 48)

        def exp_parts(x, n, r, p, s):
            step(V.tensor_scalar(n, x, 1.0 / math.log(2.0), 12582912.0, ALU.mult, ALU.add))
            step(V.tensor_scalar(n, n, -12582912.0, None, ALU.add))
            step(V.tensor_scalar(n, n, 127.0, -126.0, ALU.min, ALU.max))
            step(V.scalar_tensor_tensor(r, n, -0.693359375, x, ALU.mult, ALU.add))
            step(V.scalar_tensor_tensor(r, n, 2.12194440e-4, r, ALU.mult, ALU.add))
            step(V.tensor_scalar(p, r, 1.0 / math.factorial(9), None, ALU.mult))
            for k in range(8, 0, -1):
                step(V.scalar_tensor_tensor(p, p, 1.0 / math.factorial(k), r, ALU.add, ALU.mult))
            step(V.tensor_scalar(s.bitcast(I32), n, 127.0, 8388608.0, ALU.add, ALU.mult))

        dt = T[3][:, 0:1]
        exp_parts(T[2][:, 0:1], T[3][:, 1:2], T[3][:, 2:3], T[3][:, 3:4], T[3][:, 4:5])
        step(V.scalar_tensor_tensor(dt, T[3][:, 3:4], 1.0, T[3][:, 4:5], ALU.add, ALU.mult))
        Ar, Ai = T[0], T[1]
        X, Y, n_, r_, p_, s_ = T[4:10]
        step(V.tensor_scalar(X, Ar, dt, None, ALU.mult))
        step(V.tensor_scalar(Y, Ai, dt, None, ALU.mult))
        exp_parts(X, n_, r_, p_, s_)
        em1, ex = T[10], T[11]
        step(V.tensor_tensor(em1, p_, s_, ALU.mult))
        step(V.tensor_tensor(ex, em1, s_, ALU.add))
        step(V.scalar_tensor_tensor(em1, s_, -1.0, em1, ALU.add, ALU.add))
        step(V.tensor_scalar(n_, Y, 1.0 / (2 * math.pi), 12582912.0, ALU.mult, ALU.add))
        step(V.tensor_scalar(n_, n_, -12582912.0, None, ALU.add))
        rest = 2 * math.pi
        src = Y
        for bits in (9, 19, None):
            part = rest if bits is None else math.floor(rest * 2.0 ** (bits - 2)) / 2.0 ** (bits - 2)
            rest -= part
            step(V.scalar_tensor_tensor(r_, n_, -part, src, ALU.mult, ALU.add))
            src = r_
        hh, q_, sn, cs = T[12:16]
        step(V.tensor_scalar(hh, r_, 0.5, None, ALU.mult))
        step(V.tensor_tensor(q_, hh, hh, ALU.mult))
        step(V.tensor_scalar(sn, q_, 1.0 / math.factorial(13), None, ALU.mult))
        step(V.tensor_scalar(cs, q_, 1.0 / math.factorial(14), None, ALU.mult))
        for k in range(5, 0, -1):
            step(V.scalar_tensor_tensor(sn, sn, (-1.0) ** k / math.factorial(2 * k + 1), q_, ALU.add, ALU.mult))
        step(V.scalar_tensor_tensor(sn, sn, 1.0, hh, ALU.add, ALU.mult))
        step(V.tensor_scalar(cs, cs, -1.0, None, ALU.mult))
        for k in range(6, 0, -1):
            step(V.scalar_tensor_tensor(cs, cs, (-1.0) ** k / math.factorial(2 * k), q_, ALU.add, ALU.mult))
        step(V.tensor_scalar(cs, cs, 1.0, None, ALU.add))
        cm1 = T[16]
        step(V.scalar_tensor_tensor(cm1, sn, -2.0, sn, ALU.mult, ALU.mult))
        step(V.scalar_tensor_tensor(sn, sn, 2.0, cs, ALU.mult, ALU.mult))
        step(V.tensor_scalar(cs, cm1, 1.0, None, ALU.add))
        ar, ai, wr, wi, er, ei, rho = T[17:24]
        step(V.tensor_tensor(ar, ex, cs, ALU.mult))
        step(V.tensor_tensor(ai, ex, sn, ALU.mult))
        mr, den, t0, t1 = T[4:8]
        step(V.tensor_tensor(mr, em1, cs, ALU.mult))
        step(V.tensor_tensor(mr, mr, cm1, ALU.add))
        step(V.tensor_tensor(den, Ar, Ar, ALU.mult))
        step(V.tensor_tensor(t0, Ai, Ai, ALU.mult))
        step(V.tensor_tensor(den, den, t0, ALU.add))
        step(V.reciprocal(den, den))
        step(V.tensor_tensor(t0, mr, Ar, ALU.mult))
        step(V.tensor_tensor(t1, ai, Ai, ALU.mult))
        step(V.tensor_tensor(t0, t0, t1, ALU.add))
        step(V.tensor_tensor(wr, t0, den, ALU.mult))
        step(V.tensor_tensor(t0, ai, Ar, ALU.mult))
        step(V.tensor_tensor(t1, mr, Ai, ALU.mult))
        step(V.tensor_tensor(t0, t0, t1, ALU.subtract))
        step(V.tensor_tensor(wi, t0, den, ALU.mult))
        sc_, ss_, sr_ = cs, sn, ex
        for _ in range(3):
            step(V.tensor_tensor(t0, sc_, sc_, ALU.mult))
            step(V.tensor_tensor(t1, ss_, ss_, ALU.mult))
            step(V.scalar_tensor_tensor(ei, sc_, 2.0, ss_, ALU.mult, ALU.mult))
            step(V.tensor_tensor(er, t0, t1, ALU.subtract))
            square = V.tensor_tensor(rho, sr_, sr_, ALU.mult)
            if _ == 2:
                square.then_inc(tp_ready, 1)
            else:
                step(square)
            sc_, ss_, sr_ = er, ei, rho
            if _ < 2:
                step(V.tensor_copy(T[8], er))
                step(V.tensor_copy(T[9], ei))
                step(V.tensor_copy(T[10], rho))
                sc_, ss_, sr_ = T[8], T[9], T[10]

        def rsqrt(var, std, out, w, ch):
            ch(V.reciprocal(out, std))
            ch(V.tensor_tensor(w, out, out, ALU.mult))
            ch(V.tensor_tensor(w, w, var, ALU.mult))
            ch(V.tensor_scalar(w, w, -0.5, 1.5, ALU.mult, ALU.add))
            ch(V.tensor_tensor(out, out, w, ALU.mult))

        pre = step.n

        def norm_block(b, done, rows, dst, ch):
            st = stat[0:rows, :]
            dve.wait_ge(x_sq, done + 1)
            V.tensor_scalar(st[:, 1:2], st[:, 0:1], 1.0 / D_MODEL, EPS, ALU.mult, ALU.add).then_inc(x_var, 1)
            dve.wait_ge(x_std, done + 1)
            rsqrt(st[:, 1:2], st[:, 2:3], st[:, 3:4], st[:, 4:5], ch)
            V.scalar_tensor_tensor(xin[b][0:rows, :], xin[b][0:rows, :], st[:, 3:4], gb_bc[0:rows, :], ALU.mult, ALU.mult).then_inc(x_scaled, 1)
            for q in range(4):
                dve.wait_ge(x_hi, done * 4 + q + 1)
                s4 = acc[q % 2][:, q // 2, :].rearrange("p (k t) -> p k t", k=4)[:, :, 0:rows]
                V.tensor_tensor(XL[:, 4 * q:4 * q + 4, dst], s4, f32(XH[:, 4 * q:4 * q + 4, dst]), ALU.subtract).then_inc(x_lo, 1)

        dve.wait_ge(consts_in, 16 * (4 + NEW))
        with dve.Fori(0, 4) as r:
            for b in range(2):
                norm_block(b, 2 * r + b, P, bass.ds(r * (2 * P) + b * P, P), Chain(dve, dve_chain, r * 10 + (pre + 5 * b)))
        norm_block(0, 8, NEW, slice(SEQ, TOK), Chain(dve, dve_chain, pre + 40))
        base = pre + 45

        def split_lo(b, n1):
            dve.wait_ge(hi_ready, n1)
            V.tensor_tensor(lo[b][:, :, :], raw[b][:, :, :], f32(hi[b][:, :, :]), ALU.subtract).then_inc(lo_ready, 1)

        V.tensor_scalar(nglub[:, :], nglub[:, :], -1.0, None, ALU.mult).then_inc(dve_chain, 1)
        base += 1
        dve.wait_ge(dve_chain, base)
        split_lo(0, 1)

        with dve.Fori(0, FT) as i:
            ch = Chain(dve, dve_chain, i * DVE_A + base)

            def gate(t):
                dve.wait_ge(gate_exp, i * 6 + GATES.index(t) + 2)
                buf = szb if t == ZB else stage[stage_of(t)[0]][:, :]
                ch(V.tensor_scalar(buf, buf, 1.0, None, ALU.add))
                silu = t in (ZA, ZB)
                if silu:
                    ch(V.reciprocal(buf, buf))
                    ins = V.tensor_tensor(tok3(buf), tok3(buf), acc_v(t % 2), ALU.mult)
                else:
                    ins = V.reciprocal(buf, buf)
                ins.then_inc(szb_ready if t == ZB else stage_ready[stage_of(t)[0]], 1)
                if t == ZB:
                    dve.wait_ge(szb_ready, i + 1)
                    ch(V.tensor_copy(szb_s[:, bass.ds(i, 1), :], szb[:, SEQ:TOK].unsqueeze(1)))

            for p in range(PTS):
                if p % 4 == 0:
                    cn = p // 4 + 1
                    split_lo(cn % 2, i * CHUNKS + cn + 1)
                if p % 8 == 0 and p and p // 8 - 1 in GATES:
                    gate(p // 8 - 1)
                for hf in range(2):
                    if p == KM[hf]:
                        dve.wait_ge(k_mm, 2 * i + hf + 1)
                        V.memset(Kt[:, :, 0:7 * GC], 0.0).then_inc(kt_pad, 1)
                    if p == PQ[hf]:
                        dve.wait_ge(pq_mm, 2 * i + hf + 1)
                        dve.wait_ge(e_ready, 2 * i + hf + 1)
                        dve.wait_ge(toep_in, (i * 2 + (hf + 1)) * (16 * CH))
                        e_r, e_i = [e.rearrange("p g j -> p (g j)") for e in (Er, Ei)]
                        ch(V.tensor_tensor(T1, side[:, 0, :], e_r, ALU.mult))
                        ch(V.tensor_tensor(T2, side[:, 1, :], e_i, ALU.mult))
                        ch(V.tensor_tensor(T1, T1, T2, ALU.add))
                        for g in range(HG):
                            last = V.tensor_tensor_scan(T2[:, g * NCH:(g + 1) * NCH],
                                                        pw[:, 6 * HG + g:6 * HG + g + 1].broadcast_to([P, NCH]),
                                                        T1[:, g * NCH:(g + 1) * NCH], 0.0, ALU.mult, ALU.add)
                        ch(last)
                        T2g = T2.rearrange("p (g j) -> p g j", g=HG)
                        V.memset(V1[:, :, 0:1], 0.0)
                        V.memset(V2[:, :, 0:1], 0.0)
                        V.tensor_tensor(V1[:, :, 1:NCH + 1], Er, T2g, ALU.mult)
                        V.tensor_tensor(V2[:, :, 1:NCH + 1], Ei, T2g, ALU.mult).then_inc(v_ready, 1)
                    if p == YM[hf]:
                        dve.wait_ge(fin_copied, 2 * i + hf + 1)
                        V.tensor_tensor(hn, hA, side[:, 1, 256:256 + HG * NEW].rearrange("p (g b) -> p g b", g=HG), ALU.add).then_inc(hn_ready, 1)
                        if hf == 0:
                            dve.wait_ge(st_sent, i * 128)
                        else:
                            dve.wait_ge(st_sent, i * 128 + 64)
                        V.tensor_tensor(fo[:, 0:64], fs[:, 0:64], fs[:, 192:256], ALU.subtract)
                        V.tensor_tensor(fo[:, 64:128], fs[:, 64:128], fs[:, 128:192], ALU.add).then_inc(fin_ready, 1)
                if p == YT:
                    dve.wait_ge(yt_mm, 2 * i + 1)
                    for a in range(2):
                        yv, uv = [z[:, 0:SEQ].rearrange("p (j t) -> p t j", t=CH)[:, 4 * a:4 * a + 4, :] for z in (xy, uT)]
                        last = V.scalar_tensor_tensor(yv, uv, dcol[:, bass.ds(i, 1)], side[:, a, :].rearrange("p (t j) -> p t j", t=4), ALU.mult, ALU.add)
                    last.then_inc(yt_ready, 1)
                if p == YT + 1:
                    dve.wait_ge(yt_mm, 2 * i + 2)
                    V.scalar_tensor_tensor(xy[:, SEQ:TOK], uT[:, SEQ:TOK], dcol[:, bass.ds(i, 1)], side[:, 0, 0:NEW], ALU.mult, ALU.add).then_inc(yt_ready, 1)
                for qb in range(8):
                    w = P * (qb + 1)
                    if p == SC[qb]:
                        z = zb[qb % 2][:, 0:w]
                        dve.wait_ge(sc_mm, 8 * i + qb + 1)
                        if qb == 1:
                            dve.wait_ge(kv_sent, (i + 1) * 80)
                        V.tensor_scalar(z, side_flat[:, 0:w], SCALE, bias_all[:, bass.ds(i, 1)], ALU.mult, ALU.add).then_inc(z_ready, 1)
                        dve.wait_ge(z_ready, 8 * i + qb + 1)
                        ch(V.tensor_tensor(z[:, w - P:w], z[:, w - P:w], cmask[:, :], ALU.add))
                for qb in range(8):
                    w = P * (qb + 1)
                    if p == WT[qb] - 1:
                        dve.wait_ge(l_ready, 8 * i + qb + 1)
                        z, rv, lv = zb[qb % 2][:, 0:w], rl[:, 0:w], lk[:, 0:w]
                        ch(V.tensor_tensor_scan(rv[:, ::-1], lv[:, ::-1], rv[:, ::-1], 0.0, ALU.add, ALU.add))
                        V.tensor_tensor(z, z, rv, ALU.subtract).then_inc(arg_ready, 1)
                for qb in range(8):
                    w = P * (qb + 1)
                    if p == SC[qb]:
                        z = zb[qb % 2][:, 0:w]
                        dve.wait_ge(arg_ready, 8 * i + qb)
                        V.tensor_scalar(rl[:, 0:w], z, 0.0, None, ALU.max)
                        V.scalar_tensor_tensor(lk[:, 0:w], z, -1.0, z, ALU.mult, ALU.min).then_inc(lr_ready, 1)
                    if p == PV[qb]:
                        dve.wait_ge(pv_mm, 8 * i + qb + 1)
                        qs = szb[:, qb * P:(qb + 1) * P]
                        V.tensor_tensor(qs, qs, side[:, 0, 0:P], ALU.mult).then_inc(oz_ready, 1)
            gate(GA1)
            assert ch.n == DVE_A, ch.n
        base += FT * DVE_A
        ch = Chain(dve, dve_chain, base)

        for t in range(FT):
            dve.wait_ge(xa_ready, t + 1)
            V.tensor_tensor(XL[:, t, :], yin[t % 2], f32(XH[:, t, :]), ALU.subtract).then_inc(xb_ready, 1)
        for f in range(FT):
            split_lo((f + 1) % 2, GLU0 + f + 2)
            if f < 4:
                for b in (2 * f, 2 * f + 1):
                    dve.wait_ge(kq_done, b + 1)
                    V.tensor_reduce(Zs.rearrange("p (a n) -> p a n", a=N_PAGES)[:, :, b * HEADS:(b + 1) * HEADS],
                                    kv[b % 2].rearrange("p (a h d) -> p a h d", a=N_PAGES, h=HEADS), axis=AX.X, op=ALU.add).then_inc(zs_part, 1)
            g = stage[f % 2][:, :]
            dve.wait_ge(glu_n, f + 1)
            ch(V.tensor_scalar(g, g, 1.0, None, ALU.add))
            ch(V.reciprocal(g, g))
            dve.wait_ge(xb_ready, FT + f)
            ch(V.tensor_tensor(ysum, f32(XH[:, f, :]), f32(XL[:, f, :]), ALU.add))
            ch(V.tensor_tensor(g, g, ysum, ALU.mult))
            dve.wait_ge(sz_in[f % 2], 16 * (f // 2 + 1))
            V.tensor_tensor(g, g, sz[f % 2], ALU.mult).then_inc(y2_ready, 1)
            dve.wait_ge(xa_ready, FT + f + 1)
            V.tensor_tensor(XL[:, FT + f, :], g, f32(XH[:, FT + f, :]), ALU.subtract).then_inc(xb_ready, 1)
            if f == 4:
                dve.wait_ge(zs_tr, 1)
                ch(V.tensor_scalar(s_z, side[0:64, 0, 0:256], SCALE, bias64[:, :], ALU.mult, ALU.add))
                V.tensor_scalar(s_r, s_z, 0.0, None, ALU.max)
                V.scalar_tensor_tensor(s_l, s_z, -1.0, s_z, ALU.mult, ALU.min).then_inc(slr_ready, 1)
                dve.wait_ge(sl_ready, 2)
                ch(V.tensor_tensor_scan(s_r[:, ::-1], s_l[:, ::-1], s_r[:, ::-1], 0.0, ALU.add, ALU.add))
                V.tensor_tensor(s_z, s_z, s_r, ALU.subtract).then_inc(sarg_ready, 1)
        dve.wait_ge(spv_mm, NEW)
        V.tensor_tensor(ozs, side[:, 1, 0:64], szb_s[:, :, :].rearrange("p h b -> p (h b)"), ALU.mult).then_inc(ozs_ready, 1)
        dve.wait_ge(ozs_ready, 1)
        for t in range(HEADS):
            dve.wait_ge(xa_ready, 2 * FT + t + 1)
            V.tensor_tensor(XL[:, t, 0:SEQ], ozin[t % 4], f32(XH[:, t, 0:SEQ]), ALU.subtract)
            V.tensor_tensor(XL[:, t, SEQ:TOK], ozs[:, t * NEW:(t + 1) * NEW], f32(XH[:, t, SEQ:TOK]), ALU.subtract).then_inc(xb_ready, 1)
        with dve.Fori(0, KT // 2) as j:
            for n in range(4):
                split_lo((n + 1) % 2, j * 4 + (BR0 + n + 2))
                if n % 2:
                    b = n // 2
                    dve.wait_ge(g_in[b], j * 32 + 32)
                    dve.wait_ge(chunk_used, j * 4 + (BR0 + 2 * b + 1))
                    V.tensor_tensor(tok3(ga[b]), tok3(ga[b]), acc_v(0), ALU.mult).then_inc(br_a, 1)
                    dve.wait_ge(chunk_used, j * 4 + (BR0 + 2 * b + 2))
                    V.tensor_tensor(tok3(gb[b]), tok3(gb[b]), acc_v(1), ALU.mult).then_inc(br_b, 1)
                    dve.wait_ge(br_b, j * 2 + b + 1)
                    dve.wait_ge(stage_sent[b], j * 16 + FT * 64)
                    V.tensor_tensor(stage[b][:, :], ga[b], gb[b], ALU.add).then_inc(br_n, 1)
        for t in range(KT):
            dve.wait_ge(xa_ready, 3 * FT + t + 1)
            V.tensor_tensor(XL[:, t, :], m_in[t % MI], f32(XH[:, t, :]), ALU.subtract).then_inc(xb_ready, 1)
        dbase = base + ch.n

        def out_tiles(half, j, last, c2):
            for n in range(4):
                if not (last and n == 3):
                    split_lo((n + 1) % 2, j * 4 + (OUT0 + 32 * half + n + 2))
                if n % 2:
                    s = n // 2
                    dve.wait_ge(o_tr[s], j + 8 * half + 1)
                    dve.wait_ge(x_res, (half + 1) * 64)
                    hs = h[:, :, bass.ds(j * (2 * P) + s * P, P)]
                    V.tensor_tensor(hs, hs, side[:, s, :].rearrange("p (b f) -> p b f", b=4), ALU.add).then_inc(o_added[s], 1)
                    dve.wait_ge(o_added[s], j + 8 * half + 1)
                    sq = stage[s][:, 520:1032].rearrange("p (b f) -> p b f", b=4)
                    c2(V.tensor_tensor(sq, hs, hs, ALU.mult))
                    c2(V.tensor_reduce(ssum[:, :, bass.ds(j * 2 + s, 1)].rearrange("p b o -> p (b o)"), sq, axis=AX.X, op=ALU.add))

        def rows(half, c2):
            c2(V.tensor_reduce(hvar, ssum[:, :, :], axis=AX.X, op=ALU.add))
            V.tensor_scalar(hvar, hvar, 1.0 / D_MODEL, EPS, ALU.mult, ALU.add).then_inc(h_var, 1)
            dve.wait_ge(h_std, half + 1)
            rsqrt(hvar, stat[:, 2:6], rstd4[:, :], w4[:, :], c2)
            V.tensor_copy(w4[:, :], rstd4[:, :]).then_inc(h_rstd, 1)

        with dve.Fori(0, KT // 2) as j:
            out_tiles(0, j, False, Chain(dve, dve_chain, j * 4 + dbase))
        c2 = Chain(dve, dve_chain, dbase + 32)
        rows(0, c2)
        dbase += 32 + c2.n
        with dve.Fori(0, KT // 2 - 1) as j:
            out_tiles(1, j, False, Chain(dve, dve_chain, j * 4 + dbase))
        c2 = Chain(dve, dve_chain, dbase + 28)
        out_tiles(1, KT // 2 - 1, True, c2)
        rows(1, c2)
        dve.wait_ge(osm_tr, 1)
        dve.wait_ge(x_res, 144)
        h8 = h[0:NEW, 0, :]
        c2(V.tensor_tensor(h8[:, 0:1536], h8[:, 0:1536], acc[0][0:NEW, :, :].rearrange("p a n -> p (a n)"), ALU.add))
        c2(V.tensor_tensor(h8[:, 1536:2048], h8[:, 1536:2048], acc[1][0:NEW, 0, :], ALU.add))
        for q in range(4):
            sq = stage[0][0:NEW, 0:512]
            c2(V.tensor_tensor(sq, h8[:, q * 512:(q + 1) * 512], h8[:, q * 512:(q + 1) * 512], ALU.mult))
            c2(V.tensor_reduce(ssum[0:NEW, 0, q:q + 1], sq, axis=AX.X, op=ALU.add))
        c2(V.tensor_reduce(hvar[0:NEW, 0:1], ssum[0:NEW, 0, 0:4], axis=AX.X, op=ALU.add))
        V.tensor_scalar(hvar[0:NEW, 0:1], hvar[0:NEW, 0:1], 1.0 / D_MODEL, EPS, ALU.mult, ALU.add).then_inc(h_var, 1)
        dve.wait_ge(h_std, 3)
        rsqrt(hvar[0:NEW, 0:1], stat[0:NEW, 2:3], rstd4[0:NEW, 0:1], w4[0:NEW, 0:1], c2)
        V.tensor_copy(w4[0:NEW, :], rstd4[0:NEW, :]).then_inc(h_rstd, 1)

    @block.tensor
    def _(pe):
        mm, tr = nc.tensor.matmul, nc.tensor.transpose

        def one(out, lhsT, rhs):
            return mm(out, lhsT, rhs, start=True, stop=True)

        def x_block(b, done, rows):
            pe.wait_ge(x_scaled, done + 1)
            pe.wait_ge(x_lo, 4 * done)
            for q in range(4):
                for k in range(4):
                    last = tr(acc[q % 2][:, q // 2, k * P:k * P + rows], xin[b][0:rows, (4 * q + k) * P:(4 * q + k + 1) * P], ident[0:rows, 0:rows])
                last.then_inc(x_tr, 1)

        pe.wait_ge(pool_consts, 1)
        with pe.Fori(0, 4) as r:
            for b in range(2):
                x_block(b, 2 * r + b, P)
        x_block(0, 8, NEW)
        pe.wait_ge(tp_ready, 1)
        for n in range(7):
            src = tp[:, 64 * (17 + n):64 * (18 + n)]
            one(side[0:64, 0, n * GROUPS:(n + 1) * GROUPS], src, ident[0:64, 0:64])
            last = one(side[64:128, 0, n * GROUPS:(n + 1) * GROUPS], src, ident[0:64, 0:64])
        last.then_inc(par_t, 1)
        pe.wait_ge(x_lo, 36)

        ALL = [(a, a * NC, NC) for a in range(NB)]

        def products(b, kk, kx, s, cols, first, last):
            for w, x, start, stop in ((hi, XH, first, False), (hi, XL, False, False), (lo, XH, False, last)):
                for a, c0, n in cols:
                    ins = mm(acc[s][:, a, 0:n], w[b][:, kk, :], x[:, kx, c0:c0 + n], start=start, stop=stop)
            return ins

        def split_ready(n1):
            pe.wait_ge(hi_ready, n1)
            pe.wait_ge(lo_ready, n1)

        def acc_free(i, t):
            if t in (0, 1):
                pe.wait_ge(gate_exp, i * 6 + t)
            elif t - 2 == U:
                pe.wait_ge(u_ready, i + 1)
            elif t - 2 == ZB:
                pe.wait_ge(szb_ready, i + 1)
            elif t - 2 in (Q, K, V, ZA):
                s, m = stage_of(t - 2)
                pe.wait_ge(stage_ready[s], i * 4 + m + 1)
            else:
                pe.wait_ge(gate_exp, i * 6 + GATES.index(t - 2) + 2)

        with pe.Fori(0, FT) as i:
            for p in range(PTS):
                t, cn = p // 8, p // 4
                if p % 8 == 0:
                    acc_free(i, t)
                if p % 4 == 0:
                    split_ready(i * CHUNKS + cn + 1)
                for k in (2 * (p % 8), 2 * (p % 8) + 1):
                    last = products(cn % 2, k % CK, k, t % 2, ALL, k == 0, k == KT - 1)
                if p % 4 == 3:
                    last.then_inc(chunk_used, 1)
                for hf in range(2):
                    if p == SEED[hf]:
                        pe.wait_ge(s5_in, i * 256 + 128 * (hf + 1))
                        if hf == 0:
                            pe.wait_ge(tab_ready, 1)
                            pe.wait_ge(oz_ready, 8 * i)
                        else:
                            pe.wait_ge(ys_ready, 2 * i + 1)
                        re, im, i64, i8 = CR[:, 0:64], CR[:, 64:128], ident[0:64, 0:64], ident[0:NEW, 0:NEW]
                        for g in range(HG):
                            one(side[:, 0, 128 + g * NEW:136 + g * NEW], SR[:, g, :], i8)
                        one(side[0:64, 0, 0:64], re, i64)
                        one(side[64:128, 0, 0:64], im, negid[:, :])
                        one(side[0:64, 0, 64:128], im, negid[:, :])
                        one(side[64:128, 0, 64:128], re, negid[:, :])
                        for g in range(HG):
                            b_ = 160 + g * NEW
                            one(side[0:64, 0, b_:b_ + NEW], SR[:, g, 64:128], i8)
                            last = one(side[64:128, 0, b_:b_ + NEW], SR[:, g, 0:64], negid[0:NEW, 0:NEW])
                        last.then_inc(a_mm, 1)
                    if p == BT[hf]:
                        pe.wait_ge(m_ready, 2 * i + hf + 1)
                        pe.wait_ge(seeded, 2 * i + hf + 1)
                        for g in range(HG):
                            tr(side[:, 0, g * P:(g + 1) * P], M1[:, g, :], ident[:, :])
                            last = tr(side[:, 1, g * P:(g + 1) * P], M2[:, g, :], ident[:, :])
                        last.then_inc(b_mm, 1)
                    if p == KM[hf]:
                        pe.wait_ge(n_ready, 2 * i + hf + 1)
                        if hf == 0:
                            pe.wait_ge(us_ready, i + 1)
                        else:
                            pe.wait_ge(bt_ready, 2 * i + 2)
                        for g in range(HG):
                            last = one(side[0:GC, 0, g * P:(g + 1) * P], M1[:, g, 0:GC], N1[:, g, 0:CH * GC])
                        last.then_inc(k_mm, 1)
                    if p == PQ[hf]:
                        pe.wait_ge(kt_ready, 2 * i + hf + 1)
                        for g in range(HG):
                            one(side[:, 0, g * P:(g + 1) * P], B1T[:, g, :], Ug[:, HG * hf + g, :])
                            last = one(side[:, 1, g * P:(g + 1) * P], B2T[:, g, :], Ug[:, HG * hf + g, :])
                        last.then_inc(pq_mm, 1)
                    if p == YM[hf]:
                        pe.wait_ge(v_ready, 2 * i + hf + 1)
                        pe.wait_ge(toep_in, (i * 2 + (hf + 1)) * (16 * CH))
                        for g in range(HG):
                            out = side[:, 0, g * P:(g + 1) * P]
                            mm(out, Ug[:, HG * hf + g, :], Toep[:, g, :], start=True, stop=False)
                            mm(out, V1[:, g, 0:NCH], N1[:, g, GC:9 * GC], start=False, stop=False)
                            mm(out, V2[:, g, 0:NCH], N2[:, g, GC:9 * GC], start=False, stop=True)
                        one(side[0:HG, 1, 0:P], V1[:, :, NCH], ident[:, :])
                        one(side[0:HG, 1, P:2 * P], V2[:, :, NCH], ident[:, :])
                        for g in range(HG):
                            a = 256 + g * NEW
                            last = one(side[:, 1, a:a + NEW], B1T[0:GC, g, :], Us[:, HG * hf + g, :])
                        last.then_inc(y_mm, 1)
                    if p == YS[hf]:
                        pe.wait_ge(hn_ready, 2 * i + hf + 1)
                        pe.wait_ge(yj_ready, 2 * i + hf + 1)
                        for g in range(HG):
                            one(side[0:NEW, 1, g * GC:(g + 1) * GC], hn[:, g, :], N1[:, g, 0:GC])
                            last = one(side[0:NEW, 0, g * P:(g + 1) * P], hn[:, g, :], ident[:, :])
                        last.then_inc(ys_mm, 1)
                if p == XJ:
                    pe.wait_ge(u_ready, i + 1)
                    pe.wait_ge(bt_ready, 2 * i + 1)
                    for tau in range(CH):
                        last = tr(side_flat[:, tau * P:(tau + 1) * P], uT[:, CH - 1 - tau:SEQ:CH], ident[:, :])
                    last.then_inc(xj_mm, 1)
                if p == UG:
                    pe.wait_ge(xj_ready, i + 1)
                    for g in range(8):
                        last = tr(side_flat[:, g * P:(g + 1) * P], xy[:, g * P:(g + 1) * P], ident[:, :])
                    last.then_inc(ug_mm, 1)
                if p == US:
                    pe.wait_ge(ug_ready, i + 1)
                    for g in range(8):
                        last = one(side[0:GC, 0, g * NEW:(g + 1) * NEW], ident[:, g * GC:(g + 1) * GC], uT[:, SEQ:TOK])
                    last.then_inc(us_mm, 1)
                if p == YT:
                    pe.wait_ge(ys_ready, 2 * i + 2)
                    for tt in range(CH):
                        last = tr(side_flat[:, tt * P:(tt + 1) * P], xy[:, tt * P:(tt + 1) * P], ident[:, :])
                    last.then_inc(yt_mm, 1)
                if p == YT + 1:
                    pe.wait_ge(yt_ready, 2 * i + 1)
                    one(side[:, 0, 0:NEW], ysT, ident[0:NEW, 0:NEW]).then_inc(yt_mm, 1)
                if p == VT:
                    pe.wait_ge(at_in, i * 48 + 48)
                    pe.wait_ge(yt_ready, 2 * i + 2)
                    for kb in range(8):
                        last = tr(side_flat[:, kb * P:(kb + 1) * P], vT[:, kb * P:(kb + 1) * P], ident[:, :])
                    last.then_inc(v_tr, 1)
                if p == KTR:
                    pe.wait_ge(vtok_ready, i + 1)
                    for kb in range(8):
                        last = tr(side_flat[:, kb * P:(kb + 1) * P], kT[:, kb * P:(kb + 1) * P], ident[:, :])
                    last.then_inc(k_tr, 1)
                if p == NTR:
                    pe.wait_ge(ktok_ready, i + 1)
                    for n, src in enumerate((qT, kT, vT)):
                        last = one(side[0:NEW, 0, n * P:(n + 1) * P], src[:, SEQ:TOK], ident[:, :])
                    last.then_inc(new_tr, 1)
                for qb in range(8):
                    w = P * (qb + 1)
                    if p == SC[qb]:
                        if qb == 0:
                            pe.wait_ge(new_ready, i + 1)
                        elif qb == 1:
                            pe.wait_ge(z_ready, 8 * i + 1)
                        else:
                            pe.wait_ge(oz_ready, 8 * i + qb - 1)
                        for a in range(0, w, 512):
                            e = min(a + 512, w)
                            last = one(side_flat[:, a:e], qT[:, qb * P:(qb + 1) * P], kT[:, a:e])
                        last.then_inc(sc_mm, 1)
                for qb in range(8):
                    if p == WT[qb]:
                        pe.wait_ge(w_ready, 8 * i + qb + 1)
                        if qb < 7:
                            pe.wait_ge(z_ready, 8 * i + qb + 2)
                        else:
                            pe.wait_ge(oz_ready, 8 * i + 7)
                        for kb in range(qb + 1):
                            last = tr(side_flat[:, kb * P:(kb + 1) * P], zb[qb % 2][:, kb * P:(kb + 1) * P], ident[:, :])
                        last.then_inc(w_tr, 1)
                    if p == PV[qb]:
                        pe.wait_ge(wt_ready, 8 * i + qb + 1)
                        for kb in range(qb + 1):
                            last = mm(side[:, 0, 0:P], vtok[:, kb * P:(kb + 1) * P], wT[:, kb * P:(kb + 1) * P], start=kb == 0, stop=kb == qb)
                        last.then_inc(pv_mm, 1)

        for f in range(FT):
            if f < 2:
                pe.wait_ge(gate_exp, FT * 6 + f)
            else:
                pe.wait_ge(glu_n, f - 1)
            split_ready(GLU0 + f + 1)
            for k in range(CK):
                if f == 0:
                    pe.wait_ge(xb_ready, k + 1)
                last = products(f % 2, k, k, f % 2, ALL, k == 0, k == CK - 1)
            last.then_inc(chunk_used, 1)
            if f == 3:
                pe.wait_ge(zs_part, NEW)
                pe.wait_ge(oz_ready, 8 * FT)
                for n in range(N_PAGES):
                    last = one(side[0:64, 0, n * P:(n + 1) * P], Zs[:, n * 64:(n + 1) * 64], ident[:, :])
                last.then_inc(zs_tr, 1)
            if f == 4:
                pe.wait_ge(sw_ready, 1)
                for n in range(N_PAGES):
                    last = one(side[:, 0, n * 64:(n + 1) * 64], s_z[:, n * P:(n + 1) * P], ident[0:64, 0:64])
                last.then_inc(sw_tr, 1)
            if f >= 5:
                pe.wait_ge(swt_ready, 1)
                for b in ((0, 1, 2), (3, 4, 5), (6, 7))[f - 5]:
                    pe.wait_ge(pg_v[b % 2], 32 * (b // 2 + 1))
                    for hd in range(HEADS):
                        for n in range(N_PAGES):
                            v0 = n * WIDTH + hd * HEAD
                            last = mm(side[:, 1, hd * NEW + b:hd * NEW + b + 1], kv[b % 2][:, v0:v0 + HEAD],
                                      wsT[:, n * 64 + b * HEADS + hd:n * 64 + b * HEADS + hd + 1], start=n == 0, stop=n == N_PAGES - 1)
                    last.then_inc(spv_mm, 1)
        with pe.Fori(0, KT // 2) as j:
            for n in range(4):
                if n % 2 == 0:
                    pe.wait_ge(glu_n, FT)
                    pe.wait_ge(br_a, j * 2 + n // 2)
                    pe.wait_ge(xb_ready, 2 * FT)
                else:
                    pe.wait_ge(br_b, j * 2 + n // 2)
                    pe.wait_ge(xb_ready, 3 * FT)
                split_ready(j * 4 + (BR0 + n + 1))
                for k in range(CK):
                    last = products(n % 2, k, k + (0 if n % 2 else FT), n % 2, ALL, k == 0, k == CK - 1)
                last.then_inc(chunk_used, 1)
        pe.wait_ge(br_a, KT)
        pe.wait_ge(br_b, KT)

        def turn(half, j, s):
            pe.wait_ge(o_ready[s], j + (8 * half + 1))
            pe.wait_ge(o_added[s], j + 8 * half)
            for blk in range(4):
                last = tr(side[:, s, blk * P:(blk + 1) * P], stage[s][:, blk * P:(blk + 1) * P], ident[:, :])
            last.then_inc(o_tr[s], 1)

        for half, cols in ((0, [(0, 0, 512)]), (1, [(0, 512, 260), (1, 772, 260)])):
            with pe.Fori(0, KT // 2) as j:
                for n in range(4):
                    s = n // 2
                    if n % 2 == 0:
                        pe.wait_ge(o_ready[s], j + 8 * half)
                        pe.wait_ge(xb_ready, 3 * FT + KT)
                    split_ready(j * 4 + (OUT0 + 32 * half + n + 1))
                    for k in range(CK):
                        kx = k + CK * (n % 2)
                        last = products(n % 2, k, kx, s, cols, kx == 0, kx == KT - 1)
                    last.then_inc(chunk_used, 1)
                    if n == 2:
                        turn(half, j, 0)
                turn(half, j, 1)
        pe.wait_ge(o_ready[0], 16)
        pe.wait_ge(o_ready[1], 16)
        for f in range(KT):
            out = acc[0][0:NEW, f // 4, (f % 4) * P:(f % 4 + 1) * P] if f < 12 else acc[1][0:NEW, 0, (f - 12) * P:(f - 11) * P]
            last = one(out, outs_new[:, f, :], ident[:, :])
        last.then_inc(osm_tr, 1)


_INS = ["x_prompt", "x_sample", "cache_k", "cache_v", "state_ssm_re", "state_ssm_im", "page_table", "norm_g", "w_in",
        "ssm_A_re", "ssm_A_im", "ssm_log_dt", "ssm_B_re", "ssm_B_im", "ssm_C_re", "ssm_C_im", "ssm_D", "glu_w", "glu_b",
        "sb_bias", "w_branch_a", "w_branch_b", "w_out", "norm_f"]
_OUTS = [(1, SEQ, D_MODEL), (NEW, 1, D_MODEL), (1, 1, SEQ, HEADS, HEAD), (1, 1, SEQ, HEADS, HEAD),
         (1, NEW, 1, HEADS, HEAD), (1, NEW, 1, HEADS, HEAD), (1, 1, GROUPS, STATE), (1, 1, GROUPS, STATE),
         (1, NEW, GROUPS, STATE), (1, NEW, GROUPS, STATE)]


def kernel(**inputs):
    from contextlib import ExitStack

    import concourse.bacc as bacc
    from concourse.bass_utils import run_bass_kernel_spmd

    nc = bacc.Bacc("TRN2", target_bir_lowering=False, num_devices=1)
    arrays, args = {}, []
    for name in _INS:
        a = np.ascontiguousarray(inputs[name])
        arrays[f"in_{name}"] = a
        args.append(nc.dram_tensor(f"in_{name}", a.shape, mybir.dt.from_np(a.dtype), kind="ExternalInput").ap())
    for n, shape in enumerate(_OUTS):
        args.append(nc.dram_tensor(f"out_{n}", shape, F32, kind="ExternalOutput").ap())
    with ExitStack() as stack:
        build(stack, nc, *args)
    r = run_bass_kernel_spmd(nc, [arrays], core_ids=[0])
    return tuple(r.results[0][f"out_{n}"] for n in range(len(_OUTS)))
```

```python
import math

import numpy as np

import concourse.bass as bass
from concourse import mybir

F32 = mybir.dt.float32
F32R = mybir.dt.float32r
I32 = mybir.dt.int32
ALU = mybir.AluOpType
ACT = mybir.ActivationFunctionType
AX = mybir.AxisListType

P = 128
D_MODEL, SEQ, NEW = 2048, 1024, 8
TOK = SEQ + NEW
WIDTH = D_MODEL // 2
HEADS, HEAD = 8, 128
GROUPS, GC, STATE = 64, 16, 64
N_PAGES, PAGE = 2, 128
KT = D_MODEL // P
CK = 8
FT = WIDTH // P
NB = 3
NC = TOK // NB
CH = 8
NCH = SEQ // CH
HG = 4
EPS = 1e-6
SCALE = 1.0 / math.sqrt(HEAD)
NEG = -1e30
WORK = 10656
POOL_HALF = 133
DVE_A = 24
PRIMED = 1

TILES = 10
CHUNKS = 2 * TILES
PTS = 8 * TILES
U, ZA, GB0, Q, K, V, ZB, GB1, GA0, GA1 = range(TILES)


def weight_column(tile, i):
    at = {U: 0, ZA: 1, Q: 2, K: 3, V: 4, ZB: 5}
    if tile in at:
        return at[tile] * WIDTH + i * P
    base = 6 * WIDTH + (D_MODEL if tile in (GB0, GB1) else 0)
    return base + i * 2 * P + (P if tile in (GA1, GB1) else 0)


class Carve:

    def __init__(self, buf):
        self.buf, self.at = buf, 0

    def take(self, cols, parts=P):
        a = self.buf[0:parts, self.at:self.at + cols]
        self.at += cols
        assert self.at <= WORK, self.at
        return a


class Chain:

    def __init__(self, eng, sem, base=0):
        self.eng, self.sem, self.base, self.n = eng, sem, base, 0

    def __call__(self, *instructions):
        for ins in instructions:
            self.n += 1
            ins.then_inc(self.sem, 1)
        self.eng.wait_ge(self.sem, self.base + self.n)


def build(stack, nc, x_prompt, x_sample, cache_k, cache_v, st_re, st_im, page_table, norm_g, w_in, A_re, A_im, log_dt,
          B_re, B_im, C_re, C_im, Dw, glu_w, glu_b, sb_bias, w_a, w_b, w_out, norm_f,
          y_prompt, y_sample, k_prompt, v_prompt, k_sample, v_sample, re_prompt, im_prompt, re_sample, im_sample):
    def sb(name, shape, dt=F32):
        return nc.alloc_sbuf_tensor(name, shape, dt)

    def sem(name):
        return nc.alloc_semaphore(name)

    def dram(name, shape):
        return nc.dram_tensor(name, shape, F32, kind="Internal").ap()

    x_at = (nc.sbuf_base + 31) // 32 * 32
    XH, XL = sb("x_high", [P, KT, TOK], F32R), sb("x_low", [P, KT, TOK], F32R)
    raw = [sb(f"w_raw{b}", [P, CK, P]) for b in range(2)]
    hi = [sb(f"w_high{b}", [P, CK, P], F32R) for b in range(2)]
    lo = [sb(f"w_low{b}", [P, CK, P], F32R) for b in range(2)]
    stage = [sb(f"stage{b}", [P, TOK]) for b in range(2)]
    work = sb("work", [P, WORK])
    ident = sb("ident", [P, P])
    negid = sb("neg_ident", [64, 64])
    cmask = sb("causal_mask", [P, P])
    tab = sb("s5_tables", [P, 7, GROUPS])
    dcol, bias_all, glub = sb("d_col", [P, FT]), sb("sb_bias_all", [P, HEADS]), sb("glu_b", [P, FT])
    szb_s = sb("silu_zb_new", [P, HEADS, NEW])
    bias64 = sb("bias_rows", [HEADS * NEW, 1])
    stat = sb("norm_stats", [P, 10])
    outs_new = sb("out_new_T", [P, KT, NEW])
    ssum, hvar_t, rstd4, w4 = sb("h_squares", [P, 4, KT]), sb("h_variance", [P, 4]), sb("h_rstd", [P, 4]), sb("newton", [P, 4])
    hvar = hvar_t[:, :]
    newvar, rstd1, w1 = sb("new_variance", [P, 1]), sb("new_rstd", [P, 1]), sb("new_newton", [P, 1])
    zero1 = sb("zero1", [P, 1])
    pages = sb("pages", [1, NEW * N_PAGES], I32)
    acc = [nc.alloc_psum_tensor(f"acc{s}", [P, NB, 512], F32) for s in range(2)]
    side = nc.alloc_psum_tensor("side", [P, 2, 512], F32)
    side_flat = side[:, :, :].rearrange("p a b -> p (a b)")

    t_qkv = dram("t_qkv", [3, P, TOK])
    t_sza, t_y = dram("t_silu_za", [FT, P, TOK]), dram("t_y", [FT, P, TOK])
    t_sga, t_sgb = dram("t_sig_ga", [KT, P, TOK]), dram("t_sig_gb", [KT, P, TOK])
    t_oz, t_m = dram("t_oz", [HEADS, P, SEQ]), dram("t_merged", [KT, P, TOK])
    t_qs = dram("t_q_new", [NEW, WIDTH])

    c = Carve(work)
    xin = [c.take(D_MODEL) for _ in range(2)]
    xsq, gb_bc = c.take(D_MODEL), c.take(D_MODEL)
    tp = c.take(24 * 64, 64)

    c = Carve(work)
    uT, xy = c.take(TOK), c.take(TOK)
    Ug = c.take(8 * NCH).rearrange("p (g j) -> p g j", g=8)
    m_flat = c.take(1024)
    M1 = m_flat[:, 0:512].rearrange("p (g q) -> p g q", g=HG)
    M2 = m_flat[:, 512:1024].rearrange("p (g q) -> p g q", g=HG)
    Kt = m_flat[0:GC, 0:HG * 15 * GC].rearrange("p (g q) -> p g q", g=HG)
    T1, T2 = m_flat[:, 0:512], m_flat[:, 512:1024]
    N1 = c.take(HG * 9 * GC).rearrange("p (g q) -> p g q", g=HG)
    N2 = c.take(HG * 9 * GC).rearrange("p (g q) -> p g q", g=HG)
    Er = c.take(512).rearrange("p (g j) -> p g j", g=HG)
    Ei = c.take(512).rearrange("p (g j) -> p g j", g=HG)
    B1T = c.take(512).rearrange("p (g s) -> p g s", g=HG)
    B2T = c.take(512).rearrange("p (g s) -> p g s", g=HG)
    Toep = c.take(512).rearrange("p (g q) -> p g q", g=HG)
    v_flat = c.take(2 * HG * (NCH + 1))
    V1 = v_flat[:, 0:516].rearrange("p (g j) -> p g j", g=HG)
    V2 = v_flat[:, 516:1032].rearrange("p (g j) -> p g j", g=HG)
    PT = [v_flat[:, 256 * n:256 * n + 256] for n in range(4)]
    CR = c.take(P, 64)
    SR = c.take(HG * P, NEW).rearrange("p (g s) -> p g s", g=HG)
    SO = SR
    Bc, Bm = c.take(HG * GC), c.take(HG * GC)
    BcX, BmX = Bc.rearrange("p (g c) -> p g c", g=HG), Bm.rearrange("p (g c) -> p g c", g=HG)
    Us = c.take(8 * NEW, GC).rearrange("p (g b) -> p g b", g=8)
    h12 = c.take(2 * HG * NEW).rearrange("p (f g b) -> p f g b", f=2, g=HG)
    hA = c.take(HG * NEW).rearrange("p (g b) -> p g b", g=HG)
    hn = c.take(HG * NEW).rearrange("p (g b) -> p g b", g=HG)
    ysT = c.take(P, NEW)
    fs = c.take(2 * P, HG)
    fo = c.take(P, HG)
    pw = c.take(12 * HG)

    c = Carve(work)
    qT, kT, vT = c.take(TOK), c.take(TOK), c.take(TOK)
    wT = vT[:, 0:SEQ]
    vtok = c.take(SEQ)
    zb = [c.take(SEQ) for _ in range(2)]
    ktok = c.take(SEQ)
    lk, rl = c.take(SEQ), c.take(SEQ)
    szb = c.take(TOK)
    smp = c.take(3 * P, NEW)

    c = Carve(work)
    yin = [c.take(TOK) for _ in range(4)]
    kv = [work[:, b * 2 * WIDTH:(b + 1) * 2 * WIDTH] for b in range(2)]
    y_5th = c.at
    qbc = [c.take(WIDTH) for _ in range(2)]
    yin.append(work[:, y_5th:y_5th + TOK])
    YI = len(yin)
    sz = [c.take(TOK) for _ in range(2)]
    Zs = c.take(2 * 64)
    wsT = c.take(2 * 64)
    s_z, s_l, s_r = c.take(256, 64), c.take(256, 64), c.take(256, 64)
    ozs = c.take(HEADS * NEW)
    ysum = c.take(TOK)
    ozin = qbc + [kv[0][:, 0:SEQ], kv[0][:, SEQ:2 * SEQ]]
    PV_NEW = {(6, 0): 0, (6, 1): 1, (6, 4): 2, (6, 6): 3, (7, 1): 4, (7, 3): 5, (7, 5): 6, (7, 7): 7}

    c = Carve(work)
    ga, gb = [c.take(TOK) for _ in range(2)], [c.take(TOK) for _ in range(2)]
    MI = 6
    m_in = [c.take(TOK) for _ in range(MI)]

    c = Carve(work)
    h = c.take(4 * D_MODEL).rearrange("p (b n) -> p b n", b=4)
    nf = c.take(D_MODEL)
    over_xh = nc.alloc_sbuf_tensor_at("rows_over_x_high", [P, KT, TOK], F32, offset=x_at)
    h2 = over_xh[:, :, 0:4 * P].rearrange("p f (b n) -> p f b n", b=4)

    raw_loaded = [sem("raw_loaded0"), sem("raw_loaded1")]
    hi_ready, lo_ready, chunk_used = sem("hi_ready"), sem("lo_ready"), sem("chunk_used")
    stage_ready = [sem("stage_ready0"), sem("stage_ready1")]
    stage_sent = [sem("stage_sent0"), sem("stage_sent1")]
    consts_in = sem("consts_in")
    act_chain, pool_consts, us_mm, us_ready, br_a, br_b, h_rstd, h_scaled, h_norm_v, tp_ready = [sem(s) for s in
        ("act_chain", "pool_consts", "s5_us_mm", "s5_us_ready", "branch_a_used", "branch_b_used", "h_rstd", "h_scaled", "h_normed_dve", "tables_made")]
    x_in = [sem("x_in0"), sem("x_in1")]
    x_sq, x_var, x_std, x_scaled, x_tr, x_hi, x_lo = [sem(s) for s in
        ("x_sq", "x_var", "x_std", "x_scaled", "x_transposed", "x_hi", "x_lo")]
    dve_chain, pool_chain = sem("dve_chain"), sem("pool_chain")
    par_in, par_t, tab_ready = sem("param_in"), sem("param_T"), sem("tables_ready")
    u_ready = sem("u_ready")
    s5_in, a_mm, seeded, m_ready, n_ready, e_ready, ha_ready = [sem(s) for s in
        ("s5_in", "s5_seed_mm", "s5_seeded", "s5_m_ready", "s5_n_ready", "s5_e_ready", "s5_ha_ready")]
    b_mm, bt_ready, k_mm, kt_ready, kt_pad, toep_in = [sem(s) for s in
        ("s5_b_mm", "s5_bt_ready", "s5_k_mm", "s5_kt_ready", "s5_kt_pad", "s5_toep_in")]
    xj_mm, xj_ready, ug_mm, ug_ready, pq_mm, v_ready, y_mm, yj_ready, fin_copied, fin_ready = [sem(s) for s in
        ("s5_xj_mm", "s5_xj_ready", "s5_ug_mm", "s5_ug_ready", "s5_pq_mm", "s5_v_ready", "s5_y_mm",
         "s5_yj_ready", "s5_fin_copied", "s5_fin_ready")]
    hn_ready, ys_mm, ys_ready, yt_mm, yt_ready, y_sent, st_sent = [sem(s) for s in
        ("s5_hn_ready", "s5_ys_mm", "s5_ys_ready", "s5_yt_mm", "s5_yt_ready", "s5_y_sent", "s5_state_sent")]
    at_in, v_tr, vtok_ready, k_tr, ktok_ready, new_tr, new_ready, kv_sent = [sem(s) for s in
        ("attn_in", "v_tr", "vtok_ready", "k_tr", "ktok_ready", "new_tr", "new_ready", "kv_sent")]
    sc_mm, z_ready, lr_ready, l_ready, arg_ready, w_ready, w_tr, wt_ready, pv_mm, oz_ready, oz_sent, szb_ready = [sem(s) for s in
        ("score_mm", "z_ready", "lr_ready", "log_ready", "arg_ready", "w_ready", "w_tr", "wt_ready", "pv_mm", "oz_ready",
         "oz_sent", "szb_ready")]
    xa_ready, xb_ready = sem("act_hi_ready"), sem("act_lo_ready")
    y_in = [sem(f"y_in{n}") for n in range(YI)]
    y_gelu = sem("y_gelu")
    sz_in, y2_ready = [sem("sz_in0"), sem("sz_in1")], sem("y2_ready")
    pg_in, pg_k, pg_v, q_in = sem("pages_in"), [sem("page_k0"), sem("page_k1")], [sem("page_v0"), sem("page_v1")], [sem("q_in0"), sem("q_in1")]
    kq_done, zs_part, zs_tr, slr_ready, sl_ready, sarg_ready, sw_ready, sw_tr, swt_ready, spv_mm, ozs_ready = [sem(s) for s in
        ("kq_done", "zs_part", "zs_tr", "slr_ready", "slog_ready", "sarg_ready", "sw_ready", "sw_tr", "swt_ready",
         "spv_mm", "ozs_ready")]
    oz_in = [sem(f"oz_in{n}") for n in range(4)]
    g_in = [sem("gates_in0"), sem("gates_in1")]
    m_in_s = [sem(f"merged_in{n}") for n in range(MI)]
    x_res, nf_in, h_std, h_norm, y_out = [sem(s) for s in ("x_res", "norm_f_in", "h_std", "h_norm", "y_out")]
    o_ready, o_tr, o_added = [[sem(f"{n}{s}") for s in range(2)] for n in ("out_evacuated", "out_transposed", "out_added")]
    h_var, osm_tr, p_scaled = sem("h_var"), sem("out_new_tr"), sem("h_scaled_pool")
    glu_n, br_n = sem("glu_gate"), sem("merged_ready")

    GLU0 = FT * CHUNKS
    BR0 = GLU0 + FT
    OUT0 = BR0 + 2 * KT

    block = stack.enter_context(nc.Block())

    def f32(ap):
        return ap.bitcast(F32)

    def acc_v(s, n=NC, banks=NB):
        return acc[s][:, 0:banks, 0:n]

    def tok3(ap):
        return ap.rearrange("p (b n) -> p b n", b=NB)

    @block.sync
    def _(sp):
        for s in (oz_sent, kv_sent, at_in, st_sent, stage_sent[0], stage_sent[1]):
            sp.sem_inc(s, PRIMED)

        def load_chunk(src, k0, col, b):
            sp.dma_start(raw[b][:, :, :], src[k0 * P:(k0 + CK) * P, col].rearrange("(k p) n -> p k n", p=P)).then_inc(raw_loaded[b], 16)

        sp.dma_start(xin[0], x_prompt[0, 0:P, :]).then_inc(x_in[0], 16)
        sp.dma_start(tp[:, 0:64], A_re[0]).then_inc(par_in, 16)
        sp.dma_start(tp[:, 64:128], A_im[0]).then_inc(par_in, 16)
        sp.dma_start(tp[:, 128:129], log_dt.rearrange("a g -> g a")).then_inc(par_in, 16)
        sp.dma_start(gb_bc, norm_g[0:1, :].to_broadcast([P, D_MODEL])).then_inc(consts_in, 16)
        sp.dma_start(xin[1], x_prompt[0, P:2 * P, :]).then_inc(x_in[1], 16)
        sp.dma_start(dcol[:, :], Dw[0].rearrange("(f p) -> p f", p=P), allow_slow_non_contiguous=True).then_inc(consts_in, 16)
        sp.dma_start(glub[:, :], glu_b[0].rearrange("(f p) -> p f", p=P), allow_slow_non_contiguous=True).then_inc(consts_in, 16)
        sp.dma_start(bias_all[:, :], sb_bias[0:1, :].to_broadcast([P, HEADS])).then_inc(consts_in, 16)
        for b in range(NEW):
            sp.dma_start(bias64[b * HEADS:(b + 1) * HEADS, :], sb_bias.rearrange("a h -> h a")).then_inc(consts_in, 16)
        sp.dma_start(pages[:, :], page_table.rearrange("b n -> (b n)").unsqueeze(0)).then_inc(pg_in, 16)
        with sp.Fori(0, 3) as r:
            for b in range(2):
                sp.wait_ge(x_tr, 8 * r + 4 * b + 4)
                sp.dma_start(xin[b], x_prompt[0, bass.ds(r * (2 * P) + (2 + b) * P, P), :]).then_inc(x_in[b], 16)
        sp.wait_ge(x_tr, 28)
        sp.dma_start(xin[0][0:NEW, :], x_sample.rearrange("b o n -> (b o) n")).then_inc(x_in[0], 16)
        for b in range(2):
            load_chunk(w_in[0], b * CK, slice(0, P), b)
        sp.wait_ge(x_tr, 36)
        sp.wait_ge(par_t, 1)

        def load_y(t):
            sp.dma_start(yin[t % YI], t_y[t]).then_inc(y_in[t % YI], 16)

        def phase_a(i, last):
            if not last:
                for scale in (48, 64, 80, 128, 256, 512, 1024):
                    sp.lower_val(i * scale)
                sp.lower_val(i * P * 4)
                for primed in (i * 16, i * 48, i * 80, i * 128 + 64, i * 64 + 32, i * 64 + 48, (i + 1) * 128):
                    sp.lower_val(primed + PRIMED)
                sp.lower_val((i + 1) * 16)
                sp.lower_val((i + 1) * 128 * 4)

            def ahead(cn):
                sp.wait_ge(lo_ready, i * CHUNKS + cn + 1)
                b = cn % 2
                if cn + 2 < CHUNKS:
                    t = (cn + 2) // 2
                    load_chunk(w_in[0], b * CK, bass.ds(weight_column(t, i), P), b)
                elif not last:
                    load_chunk(w_in[0], b * CK, bass.ds(weight_column(U, i + 1), P), b)
                else:
                    load_chunk(glu_w[0], 0, slice(b * P, (b + 1) * P), b)

            def send(t):
                n = (ZA, GB0, Q, K, V, GB1, GA0, GA1).index(t)
                s, m = n % 2, n // 2
                sp.wait_ge(stage_ready[s], i * 4 + m + 1 + PRIMED)
                if t == Q:
                    sp.wait_ge(at_in, i * 48 + PRIMED)
                dst = {ZA: lambda: t_sza[bass.ds(i, 1)], Q: lambda: t_qkv[0:1], K: lambda: t_qkv[1:2],
                       V: lambda: t_qkv[2:3], GB0: lambda: t_sgb[bass.ds(2 * i, 1)],
                       GB1: lambda: t_sgb[bass.ds(2 * i + 1, 1)], GA0: lambda: t_sga[bass.ds(2 * i, 1)],
                       GA1: lambda: t_sga[bass.ds(2 * i + 1, 1)]}[t]()
                sp.dma_start(dst.rearrange("a p n -> (a p) n"), stage[s][:, :]).then_inc(stage_sent[s], 16)

            def s5_params(hf):
                if hf == 0:
                    sp.wait_ge(oz_sent, i * 16 + PRIMED)
                    sp.wait_ge(kv_sent, i * 80 + PRIMED)
                else:
                    sp.wait_ge(ha_ready, i * 2 + 1)
                    sp.wait_ge(seeded, i * 2 + 1)
                    sp.wait_ge(st_sent, i * 128 + 64 + PRIMED)
                g0 = i * (2 * HG) + hf * HG
                Bv = [x[0, bass.ds(g0, HG)].rearrange("g n c -> n g c") for x in (B_re, B_im)]
                Cv = [x[0, bass.ds(g0, HG)].rearrange("g c n -> (g c) n") for x in (C_re, C_im)]
                Sv = [x[0, :, bass.ds(g0, HG), :] for x in (st_re, st_im)]
                sp.dma_start(BcX[0:64], Bv[0]).then_inc(s5_in, 16)
                sp.dma_start(BcX[64:128], Bv[1]).then_inc(s5_in, 16)
                sp.dma_start(BmX[0:64], Bv[1]).then_inc(s5_in, 16)
                sp.dma_start(BmX[64:128], Bv[0]).then_inc(s5_in, 16)
                sp.dma_start(CR[:, 0:64], Cv[0]).then_inc(s5_in, 16)
                sp.dma_start(CR[:, 64:128], Cv[1]).then_inc(s5_in, 16)
                sp.dma_start(SR[:, :, 0:64], Sv[0]).then_inc(s5_in, 16)
                sp.dma_start(SR[:, :, 64:128], Sv[1]).then_inc(s5_in, 16)

            def toeplitz(hf):
                sp.wait_ge(kt_ready, i * 2 + hf + 1)
                sp.wait_ge(kt_pad, i * 2 + hf + 1)
                for tau in range(CH):
                    sp.dma_start(Toep[tau * GC:(tau + 1) * GC], Kt[:, :, tau * GC:(tau + CH) * GC]).then_inc(toep_in, 16)

            def s5_states(hf):
                g0 = i * (2 * HG) + hf * HG
                sp.wait_ge(fin_ready, i * 2 + hf + 1)
                for part, out in ((0, re_prompt), (1, im_prompt)):
                    sp.dma_start(out[0, 0, bass.ds(g0, HG), :], fo[:, part * 64:(part + 1) * 64]).then_inc(st_sent, 16)
                sp.wait_ge(ys_ready, i * 2 + hf + 1)
                for part, out in ((0, re_sample), (1, im_sample)):
                    sp.dma_start(out[0, :, bass.ds(g0, HG), :], SO[:, :, part * 64:(part + 1) * 64]).then_inc(st_sent, 16)

            def s5_out():
                sp.wait_ge(y_gelu, i + 1)
                sp.dma_start(t_y[bass.ds(i, 1)].rearrange("a p n -> (a p) n"), xy).then_inc(y_sent, 16)

            def attn_load():
                sp.wait_ge(y_sent, (i + 1) * 16)
                sp.wait_ge(st_sent, (i + 1) * 128 + PRIMED)
                sp.wait_ge(stage_sent[0], i * 64 + 48 + PRIMED)
                sp.wait_ge(stage_sent[1], i * 64 + 32 + PRIMED)
                for n, dst in enumerate((qT, kT, vT)):
                    sp.dma_start(dst, t_qkv[n]).then_inc(at_in, 16)

            def rows_out(ready, src, out):
                sp.wait_ge(ready, i + 1)
                sp.dma_start(out[0, 0].rearrange("(b p) h d -> p b h d", p=P)[:, :, bass.ds(i, 1), :].rearrange("p b h d -> p b (h d)"),
                             src.rearrange("p (b d) -> p b d", b=8)).then_inc(kv_sent, 16)

            def new_out():
                sp.wait_ge(new_ready, i + 1)
                sp.dma_start(t_qs[:, bass.ds(i * P, P)], smp[:, 0:P]).then_inc(kv_sent, 16)
                for n, out in ((1, k_sample), (2, v_sample)):
                    sp.dma_start(out[0, :, 0, bass.ds(i, 1), :].rearrange("b h d -> b (h d)"), smp[:, n * P:(n + 1) * P]).then_inc(kv_sent, 16)

            def oz_out():
                sp.wait_ge(oz_ready, i * 8 + 8 + PRIMED)
                sp.dma_start(t_oz[bass.ds(i, 1)].rearrange("a p n -> (a p) n"), szb[:, 0:SEQ]).then_inc(oz_sent, 16)

            for cn in range(CHUNKS):
                ahead(cn)
                if cn % 2 == 1 and cn > 1 and cn // 2 - 1 not in (U, ZB):
                    send(cn // 2 - 1)
                if cn == 0:
                    s5_params(0)
                if cn == 4:
                    toeplitz(0)
                if cn == 6:
                    s5_states(0)
                    s5_params(1)
                if cn == 10:
                    toeplitz(1)
                if cn == 12:
                    s5_states(1)
                    s5_out()
                if cn == 13:
                    attn_load()
                if cn == 15:
                    rows_out(vtok_ready, vtok, v_prompt)
                    new_out()
                if cn == 18:
                    rows_out(ktok_ready, ktok, k_prompt)
            if last:
                sp.wait_ge(sc_mm, FT * 8)
                sp.wait_ge(y_sent, FT * 16)
                load_y(0)
                load_y(1)
            oz_out()
            if last:
                for t in range(2, YI):
                    load_y(t)
            send(GA1)

        with sp.Fori(0, FT - 1) as i:
            phase_a(i, False)
        phase_a(FT - 1, True)

        sp.wait_ge(oz_sent, FT * 16 + PRIMED)
        sp.wait_ge(kv_sent, FT * 80 + PRIMED)
        sp.wait_ge(y_sent, FT * 16)
        for s in range(2):
            sp.wait_ge(stage_sent[s], FT * 64 + PRIMED)
        for b in range(2):
            sp.dma_start(sz[b], t_sza[b]).then_inc(sz_in[b], 16)
        for t in range(YI, FT):
            sp.wait_ge(xa_ready, t - YI + 1)
            sp.wait_ge(xb_ready, t - YI + 1)
            load_y(t)
        sp.wait_ge(pg_in, 16)
        sp.wait_ge(xb_ready, FT)
        sp.wait_ge(xa_ready, FT)

        def load_pages(cache, b, sems):
            for n in range(N_PAGES):
                page = sp.value_load(pages[0:1, b * N_PAGES + n:b * N_PAGES + n + 1], min_val=0,
                                     max_val=cache.shape[1] - 1)
                sp.dma_start(kv[b % 2][:, n * WIDTH:(n + 1) * WIDTH],
                             cache[0, bass.ds(page, 1)].rearrange("a t h d -> (a t) (h d)")).then_inc(sems[b % 2], 16)

        for f in range(FT):
            sp.wait_ge(lo_ready, GLU0 + f + 1)
            b = f % 2
            if f + 2 < FT:
                load_chunk(glu_w[0], 0, slice((f + 2) * P, (f + 3) * P), b)
            else:
                load_chunk((w_a, w_b)[b][0], 0, slice(0, P), b)
            if f >= 1 and f + 1 < FT:
                sp.wait_ge(y2_ready, f)
                sp.dma_start(sz[(f + 1) % 2], t_sza[f + 1]).then_inc(sz_in[(f + 1) % 2], 16)
            if f < 4:
                for bb in (2 * f, 2 * f + 1):
                    if bb >= 2:
                        sp.wait_ge(zs_part, bb - 1)
                    load_pages(cache_k, bb, pg_k)
                    sp.dma_start(qbc[bb % 2], t_qs[bb:bb + 1, :].to_broadcast([P, WIDTH])).then_inc(q_in[bb % 2], 16)
            elif f in (4, 6, 7):
                for bb in {4: (0, 1), 6: (2, 3, 4, 5), 7: (6, 7)}[f]:
                    if bb < 2:
                        sp.wait_ge(zs_part, 7 + bb)
                    else:
                        sp.wait_ge(spv_mm, bb - 1)
                    load_pages(cache_v, bb, pg_v)
            else:
                for t in range(2):
                    sp.dma_start(ozin[t], t_oz[t]).then_inc(oz_in[t], 16)
        sp.wait_ge(spv_mm, NEW - 1)
        for t in range(2, HEADS):
            if t >= 4:
                sp.wait_ge(xb_ready, 2 * FT + t - 3)
                sp.wait_ge(xa_ready, 2 * FT + t - 3)
            sp.dma_start(ozin[t % 4], t_oz[t]).then_inc(oz_in[t % 4], 16)
        sp.wait_ge(xb_ready, 3 * FT)
        sp.wait_ge(xa_ready, 3 * FT)
        sp.wait_ge(y2_ready, FT)
        for b in range(2):
            sp.dma_start(ga[b], t_sga[b]).then_inc(g_in[b], 16)
            sp.dma_start(gb[b], t_sgb[b]).then_inc(g_in[b], 16)

        def load_merged(t):
            sp.dma_start(m_in[t % MI], t_m[t]).then_inc(m_in_s[t % MI], 16)

        def branch(j, tail):
            if tail:
                for t in range(MI):
                    sp.wait_ge(stage_sent[t % 2], FT * 64 + (t // 2 + 1) * 16 + PRIMED)
                    load_merged(t)
            for b2 in range(2):
                for b in range(2):
                    sp.wait_ge(lo_ready, BR0 + 4 * j + 2 * b2 + b + 1)
                    if not (tail and b2 == 1):
                        load_chunk((w_a, w_b)[b][0], 0, bass.ds((2 * j + b2 + 1) * P, P), b)
                    else:
                        load_chunk(w_out[0], b * CK, slice(0, P), b)
            for b2 in range(2):
                sp.wait_ge(br_n, 2 * j + b2 + 1)
                sp.dma_start(t_m[bass.ds(2 * j + b2, 1)].rearrange("a p n -> (a p) n"), stage[b2][:, :]).then_inc(stage_sent[b2], 16)
                if not tail:
                    sp.dma_start(ga[b2], t_sga[bass.ds(2 * j + 2 + b2, 1)].rearrange("a p n -> (a p) n")).then_inc(g_in[b2], 16)
                    sp.dma_start(gb[b2], t_sgb[bass.ds(2 * j + 2 + b2, 1)].rearrange("a p n -> (a p) n")).then_inc(g_in[b2], 16)

        with sp.Fori(0, KT // 2 - 1) as j:
            branch(j, False)
        branch(KT // 2 - 1, True)
        for s in range(2):
            sp.wait_ge(stage_sent[s], FT * 64 + KT // 2 * 16 + PRIMED)
        for t in range(MI, KT):
            sp.wait_ge(xb_ready, 3 * FT + t - MI + 1)
            sp.wait_ge(xa_ready, 3 * FT + t - MI + 1)
            load_merged(t)
        sp.wait_ge(xb_ready, 3 * FT + KT)
        sp.wait_ge(xa_ready, 3 * FT + KT)
        for blk in range(4):
            sp.dma_start(h[:, blk, :], x_prompt[0, blk * P:(blk + 1) * P, :]).then_inc(x_res, 16)

        def out_weights(base, j, wrap, tiles=(0, 1)):
            for b2 in tiles:
                for b in range(2):
                    sp.wait_ge(lo_ready, base + 4 * j + 2 * b2 + b + 1)
                    if wrap is None or b2 == 0:
                        load_chunk(w_out[0], b * CK, bass.ds((2 * j + b2 + 1) * P, P), b)
                    elif wrap:
                        load_chunk(w_out[0], b * CK, slice(0, P), b)

        out_weights(OUT0, 0, None)
        sp.dma_start(nf, norm_f.unsqueeze(0).to_broadcast([P, D_MODEL])).then_inc(nf_in, 16)
        with sp.Fori(1, KT // 2 - 1) as j:
            out_weights(OUT0, j, None)
        out_weights(OUT0, KT // 2 - 1, True)
        out_weights(OUT0 + 32, 0, None, (0,))
        sp.wait_ge(chunk_used, OUT0 + 32 + PRIMED)
        for blk in range(4):
            sp.dma_start(h2[:, :, blk, :], x_prompt[0, (4 + blk) * P:(5 + blk) * P, :].rearrange("p (f n) -> p f n", f=KT)).then_inc(x_res, 16)
        out_weights(OUT0 + 32, 0, None, (1,))
        with sp.Fori(1, KT // 4) as j:
            out_weights(OUT0 + 32, j, None)
        for blk in range(4):
            sp.wait_ge(h_norm, blk + 1)
            sp.dma_start(y_prompt[0, blk * P:(blk + 1) * P, :], h[:, blk, :]).then_inc(y_out, 16)
        sp.wait_ge(y_out, 4 * 16)
        sp.dma_start(h[0:NEW, 0, :], x_sample.rearrange("b o n -> (b o) n")).then_inc(x_res, 16)
        with sp.Fori(KT // 4, KT // 2 - 1) as j:
            out_weights(OUT0 + 32, j, None)
        out_weights(OUT0 + 32, KT // 2 - 1, False)
        for blk in range(4):
            if blk == 0:
                sp.wait_ge(h_norm_v, 1)
            else:
                sp.wait_ge(h_norm, 4 + blk)
            sp.dma_start(y_prompt[0, (4 + blk) * P:(5 + blk) * P, :].rearrange("p (f n) -> p f n", f=KT), h2[:, :, blk, :]).then_inc(y_out, 16)
        sp.wait_ge(h_norm_v, 2)
        sp.dma_start(y_sample.rearrange("b o n -> (b o) n"), h[0:NEW, 0, :]).then_inc(y_out, 16)
        sp.wait_ge(y_out, 9 * 16)
        sp.wait_ge(kv_sent, FT * 80 + PRIMED)
        sp.wait_ge(st_sent, FT * 128 + PRIMED)

    SEED, BT, KM, PQ, YM, YS = (3, 25), (9, 33), (13, 35), (15, 37), (18, 41), (19, 42)
    XJ, UG, US, YT = 10, 11, 12, 43
    VT, NTR, KTR = 52, 53, 65
    SC = (54, 55, 58, 61, 64, 68, 72, 75)
    ST = SC[1:] + (78,)
    WT = (56, 59, 62, 66, 70, 74, 77, 79)
    PV = tuple(p + 1 for p in WT[:7]) + (79,)
    STAGED = (ZA, GB0, Q, K, V, GB1, GA0, GA1)

    def stage_of(t):
        n = STAGED.index(t)
        return n % 2, n // 2

    @block.scalar
    def _(act):
        for s in (stage_ready[0], stage_ready[1], o_ready[0], o_ready[1]):
            act.sem_inc(s, PRIMED)

        def block_rows(n):
            return (P if n < 8 else NEW), slice(n * P, n * P + (P if n < 8 else NEW))

        def squares(n):
            rows = block_rows(n)[0]
            act.wait_ge(x_in[n % 2], 16 * (n // 2 + 1))
            act.wait_ge(x_sq, n)
            nc.scalar.activation(xsq[0:rows, :], xin[n % 2][0:rows, :], ACT.Square, accum_out=stat[0:rows, 5 * (n % 2):5 * (n % 2) + 1]).then_inc(x_sq, 1)

        squares(0)
        for n in range(9):
            rows, dst = block_rows(n)
            st = stat[0:rows, 5 * (n % 2):5 * (n % 2) + 5]
            act.wait_ge(x_var, n + 1)
            nc.scalar.activation(st[:, 2:3], st[:, 1:2], ACT.Sqrt).then_inc(x_std, 1)
            if n < 8:
                squares(n + 1)
            for q in range(4):
                act.wait_ge(x_tr, n * 4 + q + 1)
                src = acc[q % 2][:, q // 2, :].rearrange("p (k t) -> p k t", k=4)[:, :, 0:rows]
                nc.scalar.copy(XH[:, 4 * q:4 * q + 4, dst], src).then_inc(x_hi, 1)
        act.wait_ge(raw_loaded[0], 16)
        nc.scalar.copy(hi[0][:, :, :], raw[0][:, :, :]).then_inc(hi_ready, 1)
        act.wait_ge(par_t, 1)
        nc.scalar.copy(tab[:, :, :], side[:, 0, 0:7 * GROUPS].rearrange("p (a g) -> p a g", a=7)).then_inc(tab_ready, 1)

        def evacuate(i, t):
            act.wait_ge(chunk_used, i * CHUNKS + 2 * (t + 1) + PRIMED)
            if t == U:
                act.wait_ge(s5_in, i * 256 + 128)
                nc.scalar.copy(tok3(uT), acc_v(0)).then_inc(u_ready, 1)
                return
            if t == ZB:
                act.wait_ge(at_in, i * 48 + 48 + PRIMED)
                nc.scalar.activation(tok3(szb), acc_v(t % 2), ACT.Silu)
                nc.scalar.activation(szb_s[:, bass.ds(i, 1), :], acc[t % 2][:, NB - 1:NB, NC - NEW:NC], ACT.Silu).then_inc(szb_ready, 1)
                return
            s, m = stage_of(t)
            act.wait_ge(stage_sent[s], i * 64 + 16 * m + PRIMED)
            if t in (Q, K, V):
                nc.scalar.copy(tok3(stage[s][:, :]), acc_v(t % 2)).then_inc(stage_ready[s], 1)
            else:
                nc.scalar.activation(tok3(stage[s][:, :]), acc_v(t % 2), ACT.Silu if t == ZA else ACT.Sigmoid).then_inc(stage_ready[s], 1)

        def split_hi(b, loaded, used):
            act.wait_ge(raw_loaded[b], loaded)
            act.wait_ge(chunk_used, used + PRIMED)
            nc.scalar.copy(hi[b][:, :, :], raw[b][:, :, :]).then_inc(hi_ready, 1)

        with act.Fori(0, FT) as i:
            for p in range(PTS):
                if p % 4 == 0:
                    cn = p // 4 + 1
                    split_hi(cn % 2, i * (CHUNKS * 8) + 16 * (cn // 2) + 16, i * CHUNKS + cn - 1)
                if p % 8 == 0 and p and p // 8 - 1 != ZB:
                    evacuate(i, p // 8 - 1)
                if p == PV[0]:
                    evacuate(i, ZB)
                for hf in range(2):
                    if p == SEED[hf]:
                        act.wait_ge(a_mm, 2 * i + hf + 1)
                        nc.scalar.copy(N1[:, :, 0:GC], side[:, 0, 0:64].rearrange("p (g c) -> p g c", g=HG))
                        nc.scalar.copy(N2[:, :, 0:GC], side[:, 0, 64:128].rearrange("p (g c) -> p g c", g=HG))
                        nc.scalar.copy(h12, side[:, 0, 128:192].rearrange("p (f g b) -> p f g b", f=2, g=HG)).then_inc(seeded, 1)
                    if p == BT[hf]:
                        act.wait_ge(b_mm, 2 * i + hf + 1)
                        nc.scalar.copy(B1T, side[:, 0, :].rearrange("p (g s) -> p g s", g=HG))
                        nc.scalar.copy(B2T, side[:, 1, :].rearrange("p (g s) -> p g s", g=HG)).then_inc(bt_ready, 1)
                    if p == KM[hf]:
                        act.wait_ge(k_mm, 2 * i + hf + 1)
                        nc.scalar.copy(Kt[:, :, 7 * GC:15 * GC], side[0:GC, 0, :].rearrange("p (g q) -> p g q", g=HG)).then_inc(kt_ready, 1)
                    if p == YM[hf]:
                        act.wait_ge(y_mm, 2 * i + hf + 1)
                        nc.scalar.copy(fs, side[0:HG, 1, 0:2 * P]).then_inc(fin_copied, 1)
                        for g in range(HG):
                            dst = xy[:, 0:SEQ].rearrange("p (t f) -> p t f", t=CH)[:, :, hf * 64 + g * GC:hf * 64 + (g + 1) * GC]
                            last = nc.scalar.copy(dst, side[:, 0, g * P:(g + 1) * P].rearrange("p (t c) -> p t c", t=CH))
                        last.then_inc(yj_ready, 1)
                    if p == YS[hf]:
                        act.wait_ge(ys_mm, 2 * i + hf + 1)
                        nc.scalar.copy(ysT[:, hf * 64:(hf + 1) * 64], side[0:NEW, 1, 0:64])
                        nc.scalar.copy(SO, side[0:NEW, 0, :].rearrange("p (g s) -> p g s", g=HG)).then_inc(ys_ready, 1)
                if p == XJ:
                    act.wait_ge(xj_mm, i + 1)
                    for tau in range(CH):
                        last = nc.scalar.copy(xy[:, 0:SEQ].rearrange("p (g t c) -> p t g c", g=8, t=CH)[:, tau],
                                              side_flat[:, tau * P:(tau + 1) * P].rearrange("p (g c) -> p g c", g=8))
                    last.then_inc(xj_ready, 1)
                if p == UG:
                    act.wait_ge(ug_mm, i + 1)
                    nc.scalar.copy(Ug, side_flat.rearrange("p (g j) -> p g j", g=8)).then_inc(ug_ready, 1)
                if p == US:
                    act.wait_ge(us_mm, i + 1)
                    nc.scalar.copy(Us, side[0:GC, 0, 0:64].rearrange("p (g b) -> p g b", g=8)).then_inc(us_ready, 1)
                if p == YT + 2:
                    act.wait_ge(yt_ready, 2 * i + 2)
                    nc.scalar.activation(xy, xy, ACT.Gelu).then_inc(y_gelu, 1)
                if p == VT:
                    act.wait_ge(v_tr, i + 1)
                    nc.scalar.copy(vtok, side_flat).then_inc(vtok_ready, 1)
                if p == KTR:
                    act.wait_ge(k_tr, i + 1)
                    nc.scalar.copy(ktok, side_flat).then_inc(ktok_ready, 1)
                if p == NTR:
                    act.wait_ge(new_tr, i + 1)
                    nc.scalar.copy(smp, side[0:NEW, 0, 0:3 * P]).then_inc(new_ready, 1)
                for qb in range(8):
                    w = P * (qb + 1)
                    if p == ST[qb]:
                        act.wait_ge(arg_ready, 8 * i + qb + 1 + PRIMED)
                        nc.scalar.activation(zb[qb % 2][:, 0:w], zb[qb % 2][:, 0:w], ACT.Exp).then_inc(w_ready, 1)
                    if p == WT[qb]:
                        act.wait_ge(w_tr, 8 * i + qb + 1)
                        nc.scalar.copy(wT[:, 0:w], side_flat[:, 0:w]).then_inc(wt_ready, 1)
                for qb in range(8):
                    w = P * (qb + 1)
                    if p == SC[qb]:
                        act.wait_ge(lr_ready, 8 * i + qb + 1)
                        nc.scalar.activation(lk[:, 0:w], lk[:, 0:w], ACT.Exp).then_inc(act_chain, 1)
                        act.wait_ge(act_chain, 8 * i + qb + 1)
                        nc.scalar.activation(lk[:, 0:w], lk[:, 0:w], ACT.Ln, bias=1.0).then_inc(l_ready, 1)
            evacuate(i, GA1)


        act.wait_ge(chunk_used, GLU0 + PRIMED)
        for t in range(FT):
            act.wait_ge(y_in[t % YI], 16 * (t // YI + 1))
            nc.scalar.copy(XH[:, t, :], yin[t % YI]).then_inc(xa_ready, 1)
        for f in range(FT):
            split_hi((f + 1) % 2, 16 * ((GLU0 + f + 1) // 2 + 1), GLU0 + f)
            act.wait_ge(chunk_used, GLU0 + f + 1 + PRIMED)
            if f < 2:
                act.wait_ge(stage_sent[f], FT * 64 + PRIMED)
            else:
                act.wait_ge(xb_ready, FT + f - 1)
            nc.scalar.activation(tok3(stage[f % 2][:, :]), acc_v(f % 2), ACT.Sigmoid, bias=glub[:, f:f + 1]).then_inc(glu_n, 1)
            if f == 4:
                act.wait_ge(slr_ready, 1)
                nc.scalar.activation(s_l, s_l, ACT.Exp).then_inc(sl_ready, 1)
                act.wait_ge(sl_ready, 1)
                nc.scalar.activation(s_l, s_l, ACT.Ln, bias=1.0).then_inc(sl_ready, 1)
                act.wait_ge(sarg_ready, 1)
                nc.scalar.activation(s_z, s_z, ACT.Exp).then_inc(sw_ready, 1)
                act.wait_ge(sw_tr, 1)
                nc.scalar.copy(wsT, side[:, 0, 0:P]).then_inc(swt_ready, 1)
            act.wait_ge(y2_ready, f + 1)
            nc.scalar.copy(XH[:, FT + f, :], stage[f % 2][:, :]).then_inc(xa_ready, 1)
        act.wait_ge(chunk_used, BR0 + PRIMED)
        act.wait_ge(y2_ready, FT)
        for t in range(HEADS):
            act.wait_ge(oz_in[t % 4], 16 * (t // 4 + 1))
            nc.scalar.copy(XH[:, t, 0:SEQ], ozin[t % 4])
            if t == 0:
                act.wait_ge(ozs_ready, 1)
            nc.scalar.copy(XH[:, t, SEQ:TOK], ozs[:, t * NEW:(t + 1) * NEW]).then_inc(xa_ready, 1)
        with act.Fori(0, KT // 2) as j:
            for n in range(4):
                split_hi((n + 1) % 2, j * 32 + 16 * (BR0 // 2 + (n + 1) // 2 + 1), j * 4 + (BR0 + n))
        act.wait_ge(chunk_used, OUT0 + PRIMED)
        for t in range(KT):
            act.wait_ge(m_in_s[t % MI], 16 * (t // MI + 1))
            nc.scalar.copy(XH[:, t, :], m_in[t % MI]).then_inc(xa_ready, 1)

        def out_steps(half, j, steps):
            for m in steps:
                split_hi((m + 1) % 2, j * 32 + 16 * (OUT0 // 2 + 16 * half + (m + 1) // 2 + 1), j * 4 + (OUT0 + 32 * half + m))
                if m % 2:
                    evacuate_out(half, j, m // 2)

        def evacuate_out(half, j, s):
            act.wait_ge(chunk_used, j * 4 + (OUT0 + 32 * half + 2 * s + 2) + PRIMED)
            act.wait_ge(o_tr[s], j + 8 * half + PRIMED)
            if half == 0:
                nc.scalar.copy(stage[s][:, 0:512], acc[s][:, 0, :]).then_inc(o_ready[s], 1)
            else:
                nc.scalar.copy(outs_new[:, bass.ds(j * 2 + s, 1), :], acc[s][:, 1, 252:260].unsqueeze(1))
                nc.scalar.copy(stage[s][:, 0:520].rearrange("p (a n) -> p a n", a=2), acc[s][:, 0:2, 0:260]).then_inc(o_ready[s], 1)

        def roots(half):
            act.wait_ge(h_var, half + 1)
            nc.scalar.activation(stat[:, 2:6], hvar, ACT.Sqrt).then_inc(h_std, 1)

        last = KT // 2 - 1
        out_steps(0, 0, (0,))
        with act.Fori(0, last) as j:
            out_steps(0, j, (1, 2, 3, 4))
        out_steps(0, last, (1, 2, 3, 4))
        roots(0)
        with act.Fori(0, last) as j:
            out_steps(1, j, (1, 2, 3, 4))
        out_steps(1, last, (1, 2))
        evacuate_out(1, last, 1)
        roots(1)
        act.wait_ge(h_rstd, 2)
        for blk in range(1, 4):
            nc.scalar.mul(h2[:, :, blk, :], h2[:, :, blk, :], rstd4[:, blk:blk + 1]).then_inc(h_scaled, 1)
        act.wait_ge(h_var, 3)
        nc.scalar.activation(stat[0:NEW, 6:7], newvar[0:NEW, :], ACT.Sqrt).then_inc(h_std, 1)

    @block.gpsimd
    def _(pool):
        nc.gpsimd.memset(zero1[:, :], 0.0).then_inc(pool_chain, 1)
        nc.gpsimd.memset(ident[:, :], 0.0).then_inc(pool_chain, 1)
        nc.gpsimd.memset(negid[:, :], 0.0).then_inc(pool_chain, 1)
        nc.gpsimd.memset(cmask[:, :], 0.0).then_inc(pool_chain, 1)
        pool.wait_ge(pool_chain, 4)
        nc.gpsimd.affine_select(out=ident[:, :], in_=ident[:, :], compare_op=ALU.not_equal, fill=1.0, base=0,
                                pattern=[[-1, P]], channel_multiplier=1)
        nc.gpsimd.affine_select(out=negid[:, :], in_=negid[:, :], compare_op=ALU.not_equal, fill=-1.0, base=0,
                                pattern=[[-1, 64]], channel_multiplier=1)
        nc.gpsimd.affine_select(out=cmask[:, :], in_=cmask[:, :], compare_op=ALU.is_gt, fill=NEG, base=0,
                                pattern=[[-1, P]], channel_multiplier=1).then_inc(pool_consts, 1)

        PER = 2 * POOL_HALF
        with pool.Fori(0, FT) as i:
            for hf in range(2):
                step = Chain(pool, pool_chain, i * PER + (4 + hf * POOL_HALF))
                pool.wait_ge(s5_in, i * 256 + 128 * (hf + 1))
                if hf == 0:
                    pool.wait_ge(tab_ready, 1)
                else:
                    pool.wait_ge(y_mm, 2 * i + 1)
                    pool.wait_ge(hn_ready, 2 * i + 1)
                pwv = pw.rearrange("p (a g) -> p a g", a=12)
                step(nc.gpsimd.tensor_copy(pwv[:, 0:7, :], tab[:, :, bass.ds(i * (2 * HG) + hf * HG, HG)]),
                     nc.gpsimd.memset(Er[:, :, 0:1], 1.0), nc.gpsimd.memset(Ei[:, :, 0:1], 0.0))
                step(nc.gpsimd.tensor_tensor(Bm[64:128, :], zero1[64:128, :].broadcast_to([64, HG * GC]), Bm[64:128, :], ALU.subtract))

                def wide(a, n):
                    return pwv[:, a, :].unsqueeze(2).broadcast_to([P, HG, n])

                def cmul(o1, o2, x1, x2, cr, ci, n, sign, done=None):
                    t = [q[:, 0:HG * n].rearrange("p (g n) -> p g n", g=HG) for q in PT]
                    step(nc.gpsimd.tensor_tensor(t[0], x1, wide(cr, n), ALU.mult),
                         nc.gpsimd.tensor_tensor(t[1], x2, wide(ci, n), ALU.mult),
                         nc.gpsimd.tensor_tensor(t[2], x2, wide(cr, n), ALU.mult),
                         nc.gpsimd.tensor_tensor(t[3], x1, wide(ci, n), ALU.mult))
                    first, second = (ALU.subtract, ALU.add) if sign > 0 else (ALU.add, ALU.subtract)
                    if done is None:
                        step(nc.gpsimd.tensor_tensor(o1, t[0], t[1], first),
                             nc.gpsimd.tensor_tensor(o2, t[2], t[3], second))
                    else:
                        step(nc.gpsimd.tensor_tensor(o1, t[0], t[1], first))
                        nc.gpsimd.tensor_tensor(o2, t[2], t[3], second).then_inc(done, 1)
                        pool.wait_ge(done, 2 * i + hf + 1)

                def square(cr, ci):
                    a, b = pwv[:, cr, :], pwv[:, ci, :]
                    step(nc.gpsimd.tensor_tensor(pwv[:, 7, :], a, a, ALU.mult),
                         nc.gpsimd.tensor_tensor(pwv[:, 8, :], b, b, ALU.mult),
                         nc.gpsimd.tensor_tensor(pwv[:, 9, :], a, b, ALU.mult))
                    step(nc.gpsimd.tensor_tensor(a, pwv[:, 7, :], pwv[:, 8, :], ALU.subtract),
                         nc.gpsimd.tensor_tensor(b, pwv[:, 9, :], pwv[:, 9, :], ALU.add))

                cmul(M1[:, :, 0:GC], M2[:, :, 0:GC], BcX, BmX, 2, 3, GC, 1)
                pool.wait_ge(seeded, 2 * i + hf + 1)
                tA = [q[:, 0:HG * NEW].rearrange("p (g b) -> p g b", g=HG) for q in PT]
                step(nc.gpsimd.tensor_tensor(tA[0], h12[:, 0], wide(0, NEW), ALU.mult),
                     nc.gpsimd.tensor_tensor(tA[1], h12[:, 1], wide(1, NEW), ALU.mult))
                nc.gpsimd.tensor_tensor(hA, tA[0], tA[1], ALU.subtract).then_inc(ha_ready, 1)
                pool.wait_ge(ha_ready, 2 * i + hf + 1)
                for n in (1, 2, 4):
                    w = n * GC
                    cmul(M1[:, :, w:2 * w], M2[:, :, w:2 * w], M1[:, :, 0:w], M2[:, :, 0:w], 0, 1, w, 1,
                         m_ready if n == 4 else None)
                    cmul(N1[:, :, w:2 * w], N2[:, :, w:2 * w], N1[:, :, 0:w], N2[:, :, 0:w], 0, 1, w, -1)
                    if n < 4:
                        square(0, 1)
                cmul(N1[:, :, 8 * GC:9 * GC], N2[:, :, 8 * GC:9 * GC], N1[:, :, 4 * GC:5 * GC], N2[:, :, 4 * GC:5 * GC], 0, 1, GC, -1,
                     n_ready)
                for k in range(7):
                    w = 1 << k
                    cmul(Er[:, :, w:2 * w], Ei[:, :, w:2 * w], Er[:, :, 0:w], Ei[:, :, 0:w], 4, 5, w, 1,
                         e_ready if k == 6 else None)
                    if k < 6:
                        square(4, 5)
                assert step.n == POOL_HALF, step.n
        for b in range(NEW):
            pool.wait_ge(pg_k[b % 2], 32 * (b // 2 + 1))
            pool.wait_ge(q_in[b % 2], 16 * (b // 2 + 1))
            kb = kv[b % 2].rearrange("p (a n) -> p a n", a=N_PAGES)
            nc.gpsimd.tensor_tensor(kb, kb, qbc[b % 2].unsqueeze(1).broadcast_to([P, N_PAGES, WIDTH]), ALU.mult).then_inc(kq_done, 1)
        pool.wait_ge(nf_in, 16)
        pool.wait_ge(h_rstd, 1)
        for blk in range(4):
            nc.gpsimd.tensor_scalar(h[:, blk, :], h[:, blk, :], rstd4[:, blk:blk + 1], None, ALU.mult).then_inc(p_scaled, 1)
        for blk in range(4):
            pool.wait_ge(p_scaled, blk + 1)
            nc.gpsimd.tensor_tensor(h[:, blk, :], h[:, blk, :], nf, ALU.mult).then_inc(h_norm, 1)
        for blk in range(1, 4):
            pool.wait_ge(h_scaled, blk)
            nc.gpsimd.tensor_tensor(h2[:, :, blk, :], h2[:, :, blk, :], nf.rearrange("p (f n) -> p f n", f=KT), ALU.mult).then_inc(h_norm, 1)

    @block.vector
    def _(dve):
        V = nc.vector
        step = Chain(dve, dve_chain)
        for s in (x_scaled, x_lo, oz_ready, br_a, br_b, arg_ready, o_added[0], o_added[1]):
            dve.sem_inc(s, PRIMED)

        T = [tp[:, 64 * n:64 * n + 64] for n in range(24)]

        def exp_parts(x, n, r, p, s):
            step(V.tensor_scalar(n, x, 1.0 / math.log(2.0), 12582912.0, ALU.mult, ALU.add))
            step(V.tensor_scalar(n, n, -12582912.0, None, ALU.add))
            step(V.tensor_scalar(n, n, 127.0, -126.0, ALU.min, ALU.max))
            step(V.scalar_tensor_tensor(r, n, -0.693359375, x, ALU.mult, ALU.add))
            step(V.scalar_tensor_tensor(r, n, 2.12194440e-4, r, ALU.mult, ALU.add))
            step(V.tensor_scalar(p, r, 1.0 / math.factorial(9), None, ALU.mult))
            for k in range(8, 0, -1):
                step(V.scalar_tensor_tensor(p, p, 1.0 / math.factorial(k), r, ALU.add, ALU.mult))
            step(V.tensor_scalar(s.bitcast(I32), n, 127.0, 8388608.0, ALU.add, ALU.mult))

        dt = T[3][:, 0:1]
        Ar, Ai = T[0], T[1]
        X, Y, n_, r_, p_, s_ = T[4:10]
        em1, ex = T[10], T[11]
        hh, q_, sn, cs = T[12:16]
        cm1 = T[16]
        ar, ai, wr, wi, er, ei, rho = T[17:24]
        mr, den, t0, t1 = T[4:8]

        def time_steps():
            exp_parts(T[2][:, 0:1], T[3][:, 1:2], T[3][:, 2:3], T[3][:, 3:4], T[3][:, 4:5])
            step(V.scalar_tensor_tensor(dt, T[3][:, 3:4], 1.0, T[3][:, 4:5], ALU.add, ALU.mult))

        def decay():
            step(V.tensor_scalar(X, Ar, dt, None, ALU.mult))
            step(V.tensor_scalar(Y, Ai, dt, None, ALU.mult))
            exp_parts(X, n_, r_, p_, s_)
            step(V.tensor_tensor(em1, p_, s_, ALU.mult))
            step(V.tensor_tensor(ex, em1, s_, ALU.add))
            step(V.scalar_tensor_tensor(em1, s_, -1.0, em1, ALU.add, ALU.add))

        def angle():
            step(V.tensor_scalar(n_, Y, 1.0 / (2 * math.pi), 12582912.0, ALU.mult, ALU.add))
            step(V.tensor_scalar(n_, n_, -12582912.0, None, ALU.add))
            rest = 2 * math.pi
            src = Y
            for bits in (9, 19, None):
                part = rest if bits is None else math.floor(rest * 2.0 ** (bits - 2)) / 2.0 ** (bits - 2)
                rest -= part
                step(V.scalar_tensor_tensor(r_, n_, -part, src, ALU.mult, ALU.add))
                src = r_
            step(V.tensor_scalar(hh, r_, 0.5, None, ALU.mult))
            step(V.tensor_tensor(q_, hh, hh, ALU.mult))

        def sine_cosine():
            step(V.tensor_scalar(sn, q_, 1.0 / math.factorial(13), None, ALU.mult))
            step(V.tensor_scalar(cs, q_, 1.0 / math.factorial(14), None, ALU.mult))
            for k in range(5, 0, -1):
                step(V.scalar_tensor_tensor(sn, sn, (-1.0) ** k / math.factorial(2 * k + 1), q_, ALU.add, ALU.mult))
            step(V.scalar_tensor_tensor(sn, sn, 1.0, hh, ALU.add, ALU.mult))
            step(V.tensor_scalar(cs, cs, -1.0, None, ALU.mult))
            for k in range(6, 0, -1):
                step(V.scalar_tensor_tensor(cs, cs, (-1.0) ** k / math.factorial(2 * k), q_, ALU.add, ALU.mult))
            step(V.tensor_scalar(cs, cs, 1.0, None, ALU.add))

        def transition():
            step(V.scalar_tensor_tensor(cm1, sn, -2.0, sn, ALU.mult, ALU.mult))
            step(V.scalar_tensor_tensor(sn, sn, 2.0, cs, ALU.mult, ALU.mult))
            step(V.tensor_scalar(cs, cm1, 1.0, None, ALU.add))
            step(V.tensor_tensor(ar, ex, cs, ALU.mult))
            step(V.tensor_tensor(ai, ex, sn, ALU.mult))
            step(V.tensor_tensor(mr, em1, cs, ALU.mult))
            step(V.tensor_tensor(mr, mr, cm1, ALU.add))
            step(V.tensor_tensor(den, Ar, Ar, ALU.mult))
            step(V.tensor_tensor(t0, Ai, Ai, ALU.mult))
            step(V.tensor_tensor(den, den, t0, ALU.add))
            step(V.reciprocal(den, den))

        def input_weight():
            step(V.tensor_tensor(t0, mr, Ar, ALU.mult))
            step(V.tensor_tensor(t1, ai, Ai, ALU.mult))
            step(V.tensor_tensor(t0, t0, t1, ALU.add))
            step(V.tensor_tensor(wr, t0, den, ALU.mult))
            step(V.tensor_tensor(t0, ai, Ar, ALU.mult))
            step(V.tensor_tensor(t1, mr, Ai, ALU.mult))
            step(V.tensor_tensor(t0, t0, t1, ALU.subtract))
            step(V.tensor_tensor(wi, t0, den, ALU.mult))

        def powers():
            sc_, ss_, sr_ = cs, sn, ex
            for _ in range(3):
                step(V.tensor_tensor(t0, sc_, sc_, ALU.mult))
                step(V.tensor_tensor(t1, ss_, ss_, ALU.mult))
                step(V.scalar_tensor_tensor(ei, sc_, 2.0, ss_, ALU.mult, ALU.mult))
                step(V.tensor_tensor(er, t0, t1, ALU.subtract))
                square = V.tensor_tensor(rho, sr_, sr_, ALU.mult)
                if _ == 2:
                    square.then_inc(tp_ready, 1)
                else:
                    step(square)
                sc_, ss_, sr_ = er, ei, rho
                if _ < 2:
                    step(V.tensor_copy(T[8], er))
                    step(V.tensor_copy(T[9], ei))
                    step(V.tensor_copy(T[10], rho))
                    sc_, ss_, sr_ = T[8], T[9], T[10]

        def rsqrt(var, std, out, w, ch):
            ch(V.reciprocal(out, std))
            ch(V.tensor_tensor(w, out, out, ALU.mult))
            ch(V.tensor_tensor(w, w, var, ALU.mult))
            ch(V.tensor_scalar(w, w, -0.5, 1.5, ALU.mult, ALU.add))
            ch(V.tensor_tensor(out, out, w, ALU.mult))

        dve.wait_ge(par_in, 48)
        parts = (time_steps, decay, angle, sine_cosine, transition, input_weight, powers)
        for n in range(9):
            rows = P if n < 8 else NEW
            dst = slice(n * P, n * P + rows)
            st, xn = stat[0:rows, 5 * (n % 2):5 * (n % 2) + 5], xin[n % 2][0:rows, :]
            dve.wait_ge(x_sq, n + 1)
            V.tensor_scalar(st[:, 1:2], st[:, 0:1], 1.0 / D_MODEL, EPS, ALU.mult, ALU.add).then_inc(x_var, 1)
            dve.wait_ge(x_std, n + 1)
            rsqrt(st[:, 1:2], st[:, 2:3], st[:, 3:4], st[:, 4:5], step)
            if n == 0:
                dve.wait_ge(consts_in, 16 * (4 + NEW))
            V.scalar_tensor_tensor(xn, xn, st[:, 3:4], gb_bc[0:rows, :], ALU.mult, ALU.mult).then_inc(x_scaled, 1)
            if n < len(parts):
                parts[n]()
            for q in range(4):
                dve.wait_ge(x_hi, n * 4 + q + 1)
                s4 = acc[q % 2][:, q // 2, :].rearrange("p (k t) -> p k t", k=4)[:, :, 0:rows]
                V.tensor_tensor(XL[:, 4 * q:4 * q + 4, dst], s4, f32(XH[:, 4 * q:4 * q + 4, dst]), ALU.subtract).then_inc(x_lo, 1)
        base = step.n

        def split_lo(b, n1):
            dve.wait_ge(hi_ready, n1)
            V.tensor_tensor(lo[b][:, :, :], raw[b][:, :, :], f32(hi[b][:, :, :]), ALU.subtract).then_inc(lo_ready, 1)

        split_lo(0, 1)

        with dve.Fori(0, FT) as i:
            ch = Chain(dve, dve_chain, i * DVE_A + base)

            for p in range(PTS):
                if p % 4 == 0:
                    cn = p // 4 + 1
                    split_lo(cn % 2, i * CHUNKS + cn + 1)
                for hf in range(2):
                    if p == KM[hf]:
                        dve.wait_ge(k_mm, 2 * i + hf + 1)
                        V.memset(Kt[:, :, 0:7 * GC], 0.0).then_inc(kt_pad, 1)
                    if p == PQ[hf]:
                        dve.wait_ge(pq_mm, 2 * i + hf + 1)
                        dve.wait_ge(e_ready, 2 * i + hf + 1)
                        dve.wait_ge(toep_in, (i * 2 + (hf + 1)) * (16 * CH))
                        e_r, e_i = [e.rearrange("p g j -> p (g j)") for e in (Er, Ei)]
                        ch(V.tensor_tensor(T1, side[:, 0, :], e_r, ALU.mult))
                        ch(V.tensor_tensor(T2, side[:, 1, :], e_i, ALU.mult))
                        ch(V.tensor_tensor(T1, T1, T2, ALU.add))
                        for g in range(HG):
                            last = V.tensor_tensor_scan(T2[:, g * NCH:(g + 1) * NCH],
                                                        pw[:, 6 * HG + g:6 * HG + g + 1].broadcast_to([P, NCH]),
                                                        T1[:, g * NCH:(g + 1) * NCH], 0.0, ALU.mult, ALU.add)
                        ch(last)
                        T2g = T2.rearrange("p (g j) -> p g j", g=HG)
                        V.memset(V1[:, :, 0:1], 0.0)
                        V.memset(V2[:, :, 0:1], 0.0)
                        V.tensor_tensor(V1[:, :, 1:NCH + 1], Er, T2g, ALU.mult)
                        V.tensor_tensor(V2[:, :, 1:NCH + 1], Ei, T2g, ALU.mult).then_inc(v_ready, 1)
                    if p == YM[hf]:
                        dve.wait_ge(fin_copied, 2 * i + hf + 1)
                        V.tensor_tensor(hn, hA, side[:, 1, 256:256 + HG * NEW].rearrange("p (g b) -> p g b", g=HG), ALU.add).then_inc(hn_ready, 1)
                        if hf == 0:
                            dve.wait_ge(st_sent, i * 128 + PRIMED)
                        else:
                            dve.wait_ge(st_sent, i * 128 + 64 + PRIMED)
                        V.tensor_tensor(fo[:, 0:64], fs[:, 0:64], fs[:, 192:256], ALU.subtract)
                        V.tensor_tensor(fo[:, 64:128], fs[:, 64:128], fs[:, 128:192], ALU.add).then_inc(fin_ready, 1)
                if p == YT:
                    dve.wait_ge(yt_mm, 2 * i + 1)
                    for a in range(2):
                        yv, uv = [z[:, 0:SEQ].rearrange("p (j t) -> p t j", t=CH)[:, 4 * a:4 * a + 4, :] for z in (xy, uT)]
                        last = V.scalar_tensor_tensor(yv, uv, dcol[:, bass.ds(i, 1)], side[:, a, :].rearrange("p (t j) -> p t j", t=4), ALU.mult, ALU.add)
                    last.then_inc(yt_ready, 1)
                if p == YT + 1:
                    dve.wait_ge(yt_mm, 2 * i + 2)
                    V.scalar_tensor_tensor(xy[:, SEQ:TOK], uT[:, SEQ:TOK], dcol[:, bass.ds(i, 1)], side[:, 0, 0:NEW], ALU.mult, ALU.add).then_inc(yt_ready, 1)
                for qb in range(8):
                    if p == PV[qb]:
                        if qb == 0:
                            dve.wait_ge(szb_ready, i + 1)
                        dve.wait_ge(pv_mm, 8 * i + qb + 1)
                        qs = szb[:, qb * P:(qb + 1) * P]
                        V.tensor_tensor(qs, qs, side[:, 0, 0:P], ALU.mult).then_inc(oz_ready, 1)
                for qb in range(8):
                    w = P * (qb + 1)
                    if p == ST[qb]:
                        dve.wait_ge(l_ready, 8 * i + qb + 1)
                        z, rv, lv = zb[qb % 2][:, 0:w], rl[:, 0:w], lk[:, 0:w]
                        ch(V.tensor_tensor_scan(rv[:, ::-1], lv[:, ::-1], rv[:, ::-1], 0.0, ALU.add, ALU.add))
                        V.tensor_tensor(z, z, rv, ALU.subtract).then_inc(arg_ready, 1)
                for qb in range(8):
                    w = P * (qb + 1)
                    if p == SC[qb]:
                        z = zb[qb % 2][:, 0:w]
                        dve.wait_ge(sc_mm, 8 * i + qb + 1)
                        V.tensor_scalar(z, side_flat[:, 0:w], SCALE, bias_all[:, bass.ds(i, 1)], ALU.mult, ALU.add).then_inc(z_ready, 1)
                        dve.wait_ge(z_ready, 8 * i + qb + 1)
                        ch(V.tensor_tensor(z[:, w - P:w], z[:, w - P:w], cmask[:, :], ALU.add))
                for qb in range(8):
                    w = P * (qb + 1)
                    if p == SC[qb]:
                        z = zb[qb % 2][:, 0:w]
                        dve.wait_ge(arg_ready, 8 * i + qb + PRIMED)
                        V.tensor_scalar(rl[:, 0:w], z, 0.0, None, ALU.max)
                        V.scalar_tensor_tensor(lk[:, 0:w], z, -1.0, z, ALU.mult, ALU.min).then_inc(lr_ready, 1)
            assert ch.n == DVE_A, ch.n
        base += FT * DVE_A
        ch = Chain(dve, dve_chain, base)

        for t in range(FT):
            dve.wait_ge(xa_ready, t + 1)
            V.tensor_tensor(XL[:, t, :], yin[t % YI], f32(XH[:, t, :]), ALU.subtract).then_inc(xb_ready, 1)
        for f in range(FT):
            split_lo((f + 1) % 2, GLU0 + f + 2)
            if f == 4:
                dve.wait_ge(zs_tr, 1)
                ch(V.tensor_scalar(s_z, side[0:64, 0, 0:256], SCALE, bias64[:, :], ALU.mult, ALU.add))
                V.tensor_scalar(s_r, s_z, 0.0, None, ALU.max)
                V.scalar_tensor_tensor(s_l, s_z, -1.0, s_z, ALU.mult, ALU.min).then_inc(slr_ready, 1)
                dve.wait_ge(sl_ready, 2)
                ch(V.tensor_tensor_scan(s_r[:, ::-1], s_l[:, ::-1], s_r[:, ::-1], 0.0, ALU.add, ALU.add))
                V.tensor_tensor(s_z, s_z, s_r, ALU.subtract).then_inc(sarg_ready, 1)
            g = stage[f % 2][:, :]
            dve.wait_ge(glu_n, f + 1)
            dve.wait_ge(sz_in[f % 2], 16 * (f // 2 + 1))
            dve.wait_ge(xb_ready, FT + f)
            ch(V.tensor_tensor(ysum, f32(XH[:, f, :]), f32(XL[:, f, :]), ALU.add))
            ch(V.tensor_tensor(g, g, ysum, ALU.mult))
            V.tensor_tensor(g, g, sz[f % 2], ALU.mult).then_inc(y2_ready, 1)
            dve.wait_ge(xa_ready, FT + f + 1)
            V.tensor_tensor(XL[:, FT + f, :], g, f32(XH[:, FT + f, :]), ALU.subtract).then_inc(xb_ready, 1)
            if f < 4:
                for b in (2 * f, 2 * f + 1):
                    dve.wait_ge(kq_done, b + 1)
                    V.tensor_reduce(Zs.rearrange("p (a n) -> p a n", a=N_PAGES)[:, :, b * HEADS:(b + 1) * HEADS],
                                    kv[b % 2].rearrange("p (a h d) -> p a h d", a=N_PAGES, h=HEADS), axis=AX.X, op=ALU.add).then_inc(zs_part, 1)
        dve.wait_ge(spv_mm, NEW)
        V.tensor_tensor(ozs, side[:, 1, 0:64], szb_s[:, :, :].rearrange("p h b -> p (h b)"), ALU.mult).then_inc(ozs_ready, 1)
        dve.wait_ge(ozs_ready, 1)
        for t in range(HEADS):
            dve.wait_ge(xa_ready, 2 * FT + t + 1)
            V.tensor_tensor(XL[:, t, 0:SEQ], ozin[t % 4], f32(XH[:, t, 0:SEQ]), ALU.subtract)
            V.tensor_tensor(XL[:, t, SEQ:TOK], ozs[:, t * NEW:(t + 1) * NEW], f32(XH[:, t, SEQ:TOK]), ALU.subtract).then_inc(xb_ready, 1)
        with dve.Fori(0, KT // 2) as j:
            for n in range(4):
                split_lo((n + 1) % 2, j * 4 + (BR0 + n + 2))
                if n % 2:
                    b = n // 2
                    dve.wait_ge(g_in[b], j * 32 + 32)
                    dve.wait_ge(chunk_used, j * 4 + (BR0 + 2 * b + 1) + PRIMED)
                    V.tensor_tensor(tok3(ga[b]), tok3(ga[b]), acc_v(0), ALU.mult).then_inc(br_a, 1)
                    dve.wait_ge(chunk_used, j * 4 + (BR0 + 2 * b + 2) + PRIMED)
                    V.tensor_tensor(tok3(gb[b]), tok3(gb[b]), acc_v(1), ALU.mult).then_inc(br_b, 1)
                    dve.wait_ge(br_b, j * 2 + b + 1 + PRIMED)
                    dve.wait_ge(stage_sent[b], j * 16 + FT * 64 + PRIMED)
                    V.tensor_tensor(stage[b][:, :], ga[b], gb[b], ALU.add).then_inc(br_n, 1)
        for t in range(KT):
            dve.wait_ge(xa_ready, 3 * FT + t + 1)
            V.tensor_tensor(XL[:, t, :], m_in[t % MI], f32(XH[:, t, :]), ALU.subtract).then_inc(xb_ready, 1)
        dbase = base + ch.n

        def out_steps(half, j, steps, c2):
            for m in steps:
                split_lo((m + 1) % 2, j * 4 + (OUT0 + 32 * half + m + 2))
                if m in (2, 4):
                    add_rows(half, j, m // 2 - 1, c2)

        def add_rows(half, j, s, c2):
            dve.wait_ge(o_tr[s], j + (8 * half + 1) + PRIMED)
            dve.wait_ge(x_res, (half + 1) * 64)
            if half == 0:
                hs = h[:, :, bass.ds(j * (2 * P) + s * P, P)]
            else:
                hs = h2[:, bass.ds(j * 2 + s, 1)].rearrange("p f b n -> p (f b) n")
            V.tensor_tensor(hs, hs, side[:, s, :].rearrange("p (b f) -> p b f", b=4), ALU.add).then_inc(o_added[s], 1)
            dve.wait_ge(o_added[s], j + (8 * half + 1) + PRIMED)
            sq = stage[s][:, 520:1032].rearrange("p (b f) -> p b f", b=4)
            c2(V.tensor_tensor(sq, hs, hs, ALU.mult))
            c2(V.tensor_reduce(ssum[:, :, bass.ds(j * 2 + s, 1)].rearrange("p b o -> p (b o)"), sq, axis=AX.X, op=ALU.add))

        def variance(c2):
            c2(V.tensor_reduce(hvar, ssum[:, :, :], axis=AX.X, op=ALU.add))
            V.tensor_scalar(hvar, hvar, 1.0 / D_MODEL, EPS, ALU.mult, ALU.add).then_inc(h_var, 1)

        def inverse_roots(half, c2):
            dve.wait_ge(h_std, half + 1)
            rsqrt(hvar, stat[:, 2:6], rstd4[:, :], w4[:, :], c2)
            V.tensor_copy(w4[:, :], rstd4[:, :]).then_inc(h_rstd, 1)

        last = KT // 2 - 1
        out_steps(0, 0, (0,), None)
        with dve.Fori(0, last) as j:
            out_steps(0, j, (1, 2, 3, 4), Chain(dve, dve_chain, j * 4 + dbase))
        c2 = Chain(dve, dve_chain, dbase + 4 * last)
        out_steps(0, last, (1, 2, 3, 4), c2)
        variance(c2)
        inverse_roots(0, c2)
        dbase += 4 * last + c2.n
        with dve.Fori(0, last) as j:
            out_steps(1, j, (1, 2, 3, 4), Chain(dve, dve_chain, j * 4 + dbase))
        c2 = Chain(dve, dve_chain, dbase + 4 * last)
        out_steps(1, last, (1, 2), c2)
        add_rows(1, last, 1, c2)
        variance(c2)
        inverse_roots(1, c2)
        rows = h2[:, :, 0, :]
        V.scalar_tensor_tensor(rows, rows, rstd4[:, 0:1], nf.rearrange("p (f n) -> p f n", f=KT), ALU.mult, ALU.mult).then_inc(h_norm_v, 1)
        dve.wait_ge(osm_tr, 1)
        dve.wait_ge(x_res, 144)
        h8 = h[0:NEW, 0, :]
        c2(V.tensor_tensor(h8[:, 0:1536], h8[:, 0:1536], acc[0][0:NEW, :, :].rearrange("p a n -> p (a n)"), ALU.add),
           V.tensor_tensor(h8[:, 1536:2048], h8[:, 1536:2048], acc[1][0:NEW, 0, :], ALU.add))
        sq = stage[0][0:NEW, 0:512]
        for q in range(4):
            c2(V.tensor_tensor(sq, h8[:, q * 512:(q + 1) * 512], h8[:, q * 512:(q + 1) * 512], ALU.mult))
            c2(V.tensor_reduce(ssum[0:NEW, 0, q:q + 1], sq, axis=AX.X, op=ALU.add))
        n8 = newvar[0:NEW, :]
        c2(V.tensor_reduce(n8, ssum[0:NEW, 0, 0:4], axis=AX.X, op=ALU.add))
        V.tensor_scalar(n8, n8, 1.0 / D_MODEL, EPS, ALU.mult, ALU.add).then_inc(h_var, 1)
        dve.wait_ge(h_std, 3)
        rsqrt(n8, stat[0:NEW, 6:7], rstd1[0:NEW, :], w1[0:NEW, :], c2)
        V.scalar_tensor_tensor(h8, h8, rstd1[0:NEW, :], nf[0:NEW, :], ALU.mult, ALU.mult).then_inc(h_norm_v, 1)

    @block.tensor
    def _(pe):
        mm, tr = nc.tensor.matmul, nc.tensor.transpose
        for s in (chunk_used, o_tr[0], o_tr[1]):
            pe.sem_inc(s, PRIMED)

        def one(out, lhsT, rhs):
            return mm(out, lhsT, rhs, start=True, stop=True)

        def x_block(b, done, rows):
            pe.wait_ge(x_scaled, done + 1 + PRIMED)
            pe.wait_ge(x_lo, 4 * done + PRIMED)
            for q in range(4):
                for k in range(4):
                    last = tr(acc[q % 2][:, q // 2, k * P:k * P + rows], xin[b][0:rows, (4 * q + k) * P:(4 * q + k + 1) * P], ident[0:rows, 0:rows])
                last.then_inc(x_tr, 1)

        pe.wait_ge(pool_consts, 1)
        with pe.Fori(0, 4) as r:
            for b in range(2):
                x_block(b, 2 * r + b, P)
        x_block(0, 8, NEW)
        pe.wait_ge(tp_ready, 1)
        for n in range(7):
            src = tp[:, 64 * (17 + n):64 * (18 + n)]
            one(side[0:64, 0, n * GROUPS:(n + 1) * GROUPS], src, ident[0:64, 0:64])
            last = one(side[64:128, 0, n * GROUPS:(n + 1) * GROUPS], src, ident[0:64, 0:64])
        last.then_inc(par_t, 1)
        pe.wait_ge(x_lo, 36 + PRIMED)

        ALL = [(a, a * NC, NC) for a in range(NB)]

        def products(b, kk, kx, s, cols, first, last):
            for w, x, start, stop in ((hi, XH, first, False), (hi, XL, False, False), (lo, XH, False, last)):
                for a, c0, n in cols:
                    ins = mm(acc[s][:, a, 0:n], w[b][:, kk, :], x[:, kx, c0:c0 + n], start=start, stop=stop)
            return ins

        def split_ready(n1):
            pe.wait_ge(hi_ready, n1)
            pe.wait_ge(lo_ready, n1)

        def acc_free(i, t):
            if t in (0, 1):
                pe.wait_ge(stage_ready[t], i * 4 + PRIMED)
            elif t - 2 == U:
                pe.wait_ge(u_ready, i + 1)
            elif t - 2 == ZB:
                pe.wait_ge(szb_ready, i + 1)
            else:
                s, m = stage_of(t - 2)
                pe.wait_ge(stage_ready[s], i * 4 + m + 1 + PRIMED)

        with pe.Fori(0, FT) as i:
            for p in range(PTS):
                t, cn = p // 8, p // 4
                if p % 8 == 0:
                    acc_free(i, t)
                if p % 4 == 0:
                    split_ready(i * CHUNKS + cn + 1)
                for k in (2 * (p % 8), 2 * (p % 8) + 1):
                    last = products(cn % 2, k % CK, k, t % 2, ALL, k == 0, k == KT - 1)
                if p % 4 == 3:
                    last.then_inc(chunk_used, 1)
                for hf in range(2):
                    if p == SEED[hf]:
                        pe.wait_ge(s5_in, i * 256 + 128 * (hf + 1))
                        if hf == 0:
                            pe.wait_ge(tab_ready, 1)
                            pe.wait_ge(oz_ready, 8 * i + PRIMED)
                        else:
                            pe.wait_ge(ys_ready, 2 * i + 1)
                        re, im, i64, i8 = CR[:, 0:64], CR[:, 64:128], ident[0:64, 0:64], ident[0:NEW, 0:NEW]
                        for g in range(HG):
                            one(side[:, 0, 128 + g * NEW:136 + g * NEW], SR[:, g, :], i8)
                        one(side[0:64, 0, 0:64], re, i64)
                        one(side[64:128, 0, 0:64], im, negid[:, :])
                        one(side[0:64, 0, 64:128], im, negid[:, :])
                        one(side[64:128, 0, 64:128], re, negid[:, :])
                        for g in range(HG):
                            b_ = 160 + g * NEW
                            one(side[0:64, 0, b_:b_ + NEW], SR[:, g, 64:128], i8)
                            last = one(side[64:128, 0, b_:b_ + NEW], SR[:, g, 0:64], negid[0:NEW, 0:NEW])
                        last.then_inc(a_mm, 1)
                    if p == BT[hf]:
                        pe.wait_ge(m_ready, 2 * i + hf + 1)
                        pe.wait_ge(seeded, 2 * i + hf + 1)
                        for g in range(HG):
                            tr(side[:, 0, g * P:(g + 1) * P], M1[:, g, :], ident[:, :])
                            last = tr(side[:, 1, g * P:(g + 1) * P], M2[:, g, :], ident[:, :])
                        last.then_inc(b_mm, 1)
                    if p == KM[hf]:
                        pe.wait_ge(n_ready, 2 * i + hf + 1)
                        if hf == 0:
                            pe.wait_ge(us_ready, i + 1)
                        else:
                            pe.wait_ge(bt_ready, 2 * i + 2)
                        for g in range(HG):
                            last = one(side[0:GC, 0, g * P:(g + 1) * P], M1[:, g, 0:GC], N1[:, g, 0:CH * GC])
                        last.then_inc(k_mm, 1)
                    if p == PQ[hf]:
                        pe.wait_ge(kt_ready, 2 * i + hf + 1)
                        for g in range(HG):
                            one(side[:, 0, g * P:(g + 1) * P], B1T[:, g, :], Ug[:, HG * hf + g, :])
                            last = one(side[:, 1, g * P:(g + 1) * P], B2T[:, g, :], Ug[:, HG * hf + g, :])
                        last.then_inc(pq_mm, 1)
                    if p == YM[hf]:
                        pe.wait_ge(v_ready, 2 * i + hf + 1)
                        pe.wait_ge(toep_in, (i * 2 + (hf + 1)) * (16 * CH))
                        for g in range(HG):
                            out = side[:, 0, g * P:(g + 1) * P]
                            mm(out, Ug[:, HG * hf + g, :], Toep[:, g, :], start=True, stop=False)
                            mm(out, V1[:, g, 0:NCH], N1[:, g, GC:9 * GC], start=False, stop=False)
                            mm(out, V2[:, g, 0:NCH], N2[:, g, GC:9 * GC], start=False, stop=True)
                        one(side[0:HG, 1, 0:P], V1[:, :, NCH], ident[:, :])
                        one(side[0:HG, 1, P:2 * P], V2[:, :, NCH], ident[:, :])
                        for g in range(HG):
                            a = 256 + g * NEW
                            last = one(side[:, 1, a:a + NEW], B1T[0:GC, g, :], Us[:, HG * hf + g, :])
                        last.then_inc(y_mm, 1)
                    if p == YS[hf]:
                        pe.wait_ge(hn_ready, 2 * i + hf + 1)
                        pe.wait_ge(yj_ready, 2 * i + hf + 1)
                        for g in range(HG):
                            one(side[0:NEW, 1, g * GC:(g + 1) * GC], hn[:, g, :], N1[:, g, 0:GC])
                            last = one(side[0:NEW, 0, g * P:(g + 1) * P], hn[:, g, :], ident[:, :])
                        last.then_inc(ys_mm, 1)
                if p == XJ:
                    pe.wait_ge(u_ready, i + 1)
                    pe.wait_ge(bt_ready, 2 * i + 1)
                    for tau in range(CH):
                        last = tr(side_flat[:, tau * P:(tau + 1) * P], uT[:, CH - 1 - tau:SEQ:CH], ident[:, :])
                    last.then_inc(xj_mm, 1)
                if p == UG:
                    pe.wait_ge(xj_ready, i + 1)
                    for g in range(8):
                        last = tr(side_flat[:, g * P:(g + 1) * P], xy[:, g * P:(g + 1) * P], ident[:, :])
                    last.then_inc(ug_mm, 1)
                if p == US:
                    pe.wait_ge(ug_ready, i + 1)
                    for g in range(8):
                        last = one(side[0:GC, 0, g * NEW:(g + 1) * NEW], ident[:, g * GC:(g + 1) * GC], uT[:, SEQ:TOK])
                    last.then_inc(us_mm, 1)
                if p == YT:
                    pe.wait_ge(ys_ready, 2 * i + 2)
                    for tt in range(CH):
                        last = tr(side_flat[:, tt * P:(tt + 1) * P], xy[:, tt * P:(tt + 1) * P], ident[:, :])
                    last.then_inc(yt_mm, 1)
                if p == YT + 1:
                    pe.wait_ge(yt_ready, 2 * i + 1)
                    one(side[:, 0, 0:NEW], ysT, ident[0:NEW, 0:NEW]).then_inc(yt_mm, 1)
                if p == VT:
                    pe.wait_ge(at_in, i * 48 + 48 + PRIMED)
                    pe.wait_ge(yt_ready, 2 * i + 2)
                    for kb in range(8):
                        last = tr(side_flat[:, kb * P:(kb + 1) * P], vT[:, kb * P:(kb + 1) * P], ident[:, :])
                    last.then_inc(v_tr, 1)
                if p == KTR:
                    pe.wait_ge(z_ready, 8 * i + 5)
                    for kb in range(8):
                        last = tr(side_flat[:, kb * P:(kb + 1) * P], kT[:, kb * P:(kb + 1) * P], ident[:, :])
                    last.then_inc(k_tr, 1)
                if p == NTR:
                    pe.wait_ge(vtok_ready, i + 1)
                    for n, src in enumerate((qT, kT, vT)):
                        last = one(side[0:NEW, 0, n * P:(n + 1) * P], src[:, SEQ:TOK], ident[:, :])
                    last.then_inc(new_tr, 1)
                for qb in range(8):
                    if p == WT[qb]:
                        pe.wait_ge(w_ready, 8 * i + qb + 1)
                        if qb == 3:
                            pe.wait_ge(ktok_ready, i + 1)
                        elif qb < 7:
                            pe.wait_ge(z_ready, 8 * i + qb + 2)
                        else:
                            pe.wait_ge(oz_ready, 8 * i + 7 + PRIMED)
                        for kb in range(qb + 1):
                            last = tr(side_flat[:, kb * P:(kb + 1) * P], zb[qb % 2][:, kb * P:(kb + 1) * P], ident[:, :])
                        last.then_inc(w_tr, 1)
                    if p == PV[qb]:
                        pe.wait_ge(wt_ready, 8 * i + qb + 1)
                        for kb in range(qb + 1):
                            last = mm(side[:, 0, 0:P], vtok[:, kb * P:(kb + 1) * P], wT[:, kb * P:(kb + 1) * P], start=kb == 0, stop=kb == qb)
                        last.then_inc(pv_mm, 1)
                for qb in range(8):
                    w = P * (qb + 1)
                    if p == SC[qb]:
                        if qb == 0:
                            pe.wait_ge(new_ready, i + 1)
                        elif qb == 1:
                            pe.wait_ge(z_ready, 8 * i + 1)
                        else:
                            pe.wait_ge(oz_ready, 8 * i + qb - 1 + PRIMED)
                        for a in range(0, w, 512):
                            e = min(a + 512, w)
                            last = one(side_flat[:, a:e], qT[:, qb * P:(qb + 1) * P], kT[:, a:e])
                        last.then_inc(sc_mm, 1)

        for f in range(FT):
            if f < 2:
                pe.wait_ge(stage_ready[f], FT * 4 + PRIMED)
            else:
                pe.wait_ge(glu_n, f - 1)
            split_ready(GLU0 + f + 1)
            for k in range(CK):
                if f == 0:
                    pe.wait_ge(xb_ready, k + 1)
                last = products(f % 2, k, k, f % 2, ALL, k == 0, k == CK - 1)
                if k == CK - 1:
                    last.then_inc(chunk_used, 1)
                if (f, k) == (4, CK - 1):
                    pe.wait_ge(zs_part, NEW)
                    pe.wait_ge(oz_ready, 8 * FT + PRIMED)
                    for n in range(N_PAGES):
                        last = one(side[0:64, 0, n * P:(n + 1) * P], Zs[:, n * 64:(n + 1) * 64], ident[:, :])
                    last.then_inc(zs_tr, 1)
                if (f, k) == (5, 6):
                    pe.wait_ge(sw_ready, 1)
                    for n in range(N_PAGES):
                        last = one(side[:, 0, n * 64:(n + 1) * 64], s_z[:, n * P:(n + 1) * P], ident[0:64, 0:64])
                    last.then_inc(sw_tr, 1)
                if (f, k) in PV_NEW:
                    b = PV_NEW[f, k]
                    pe.wait_ge(swt_ready, 1)
                    pe.wait_ge(pg_v[b % 2], 32 * (b // 2 + 1))
                    for hd in range(HEADS):
                        for n in range(N_PAGES):
                            v0 = n * WIDTH + hd * HEAD
                            last = mm(side[:, 1, hd * NEW + b:hd * NEW + b + 1], kv[b % 2][:, v0:v0 + HEAD],
                                      wsT[:, n * 64 + b * HEADS + hd:n * 64 + b * HEADS + hd + 1], start=n == 0, stop=n == N_PAGES - 1)
                    last.then_inc(spv_mm, 1)
        with pe.Fori(0, KT // 2) as j:
            for n in range(4):
                if n % 2 == 0:
                    pe.wait_ge(glu_n, FT)
                    pe.wait_ge(br_a, j * 2 + n // 2 + PRIMED)
                else:
                    pe.wait_ge(br_b, j * 2 + n // 2 + PRIMED)
                split_ready(j * 4 + (BR0 + n + 1))
                for k in range(CK):
                    if n < 2:
                        pe.wait_ge(xb_ready, (1 + n) * FT + k + 1)
                    last = products(n % 2, k, k + (0 if n % 2 else FT), n % 2, ALL, k == 0, k == CK - 1)
                last.then_inc(chunk_used, 1)
        pe.wait_ge(br_a, KT + PRIMED)
        pe.wait_ge(br_b, KT + PRIMED)

        def turn(half, j, s):
            pe.wait_ge(o_ready[s], j + (8 * half + 1) + PRIMED)
            pe.wait_ge(o_added[s], j + 8 * half + PRIMED)
            for blk in range(4):
                last = tr(side[:, s, blk * P:(blk + 1) * P], stage[s][:, blk * P:(blk + 1) * P], ident[:, :])
            last.then_inc(o_tr[s], 1)

        HALF_COLS = ([(0, 0, 512)], [(0, 512, 260), (1, 772, 260)])

        def out_chunk(half, j, m):
            s = m // 2 % 2
            if m % 2 == 0:
                pe.wait_ge(o_ready[s], j + (m // 4) + 8 * half + PRIMED)
            split_ready(j * 4 + (OUT0 + 32 * half + m + 1))
            for k in range(CK):
                kx = k + CK * (m % 2)
                if half == 0 and m < 2:
                    pe.wait_ge(xb_ready, 3 * FT + kx + 1)
                ins = products(m % 2, k, kx, s, HALF_COLS[half], kx == 0, kx == KT - 1)
            ins.then_inc(chunk_used, 1)

        def out_pair(half, j, following):
            out_chunk(half, j, 1)
            out_chunk(half, j, 2)
            turn(half, j, 0)
            out_chunk(half, j, 3)
            if following is not None:
                out_chunk(*following)
            turn(half, j, 1)

        last_pair = KT // 2 - 1
        out_chunk(0, 0, 0)
        with pe.Fori(0, last_pair) as j:
            out_pair(0, j, (0, j, 4))
        out_pair(0, last_pair, (1, 0, 0))
        with pe.Fori(0, last_pair) as j:
            out_pair(1, j, (1, j, 4))
        out_pair(1, last_pair, None)
        pe.wait_ge(o_ready[0], 16 + PRIMED)
        pe.wait_ge(o_ready[1], 16 + PRIMED)
        for f in range(KT):
            out = acc[0][0:NEW, f // 4, (f % 4) * P:(f % 4 + 1) * P] if f < 12 else acc[1][0:NEW, 0, (f - 12) * P:(f - 11) * P]
            last = one(out, outs_new[:, f, :], ident[:, :])
        last.then_inc(osm_tr, 1)


_INS = ["x_prompt", "x_sample", "cache_k", "cache_v", "state_ssm_re", "state_ssm_im", "page_table", "norm_g", "w_in",
        "ssm_A_re", "ssm_A_im", "ssm_log_dt", "ssm_B_re", "ssm_B_im", "ssm_C_re", "ssm_C_im", "ssm_D", "glu_w", "glu_b",
        "sb_bias", "w_branch_a", "w_branch_b", "w_out", "norm_f"]
_OUTS = [(1, SEQ, D_MODEL), (NEW, 1, D_MODEL), (1, 1, SEQ, HEADS, HEAD), (1, 1, SEQ, HEADS, HEAD),
         (1, NEW, 1, HEADS, HEAD), (1, NEW, 1, HEADS, HEAD), (1, 1, GROUPS, STATE), (1, 1, GROUPS, STATE),
         (1, NEW, GROUPS, STATE), (1, NEW, GROUPS, STATE)]


def kernel(**inputs):
    from contextlib import ExitStack

    import concourse.bacc as bacc
    from concourse.bass_utils import run_bass_kernel_spmd

    nc = bacc.Bacc("TRN2", target_bir_lowering=False, num_devices=1)
    arrays, args = {}, []
    for name in _INS:
        a = np.ascontiguousarray(inputs[name])
        arrays[f"in_{name}"] = a
        args.append(nc.dram_tensor(f"in_{name}", a.shape, mybir.dt.from_np(a.dtype), kind="ExternalInput").ap())
    for n, shape in enumerate(_OUTS):
        args.append(nc.dram_tensor(f"out_{n}", shape, F32, kind="ExternalOutput").ap())
    with ExitStack() as stack:
        build(stack, nc, *args)
    r = run_bass_kernel_spmd(nc, [arrays], core_ids=[0])
    return tuple(r.results[0][f"out_{n}"] for n in range(len(_OUTS)))
```
